# Optimizing a Trainium2 kernel written in Bass

```python
import math
import jax
import jax.numpy as jnp
from jax import lax
import numpy as np

D_MODEL = 1024
BATCH = 1
SEQ = 256
DEPTH = 2

GROUP_WIDTH = D_MODEL // 2
D_MIX = 3 * GROUP_WIDTH
ATTN_HEADS = 4
ATTN_HEAD_DIM = GROUP_WIDTH // (2 * ATTN_HEADS)
Q_BLOCK = 128
SSD_HEAD_DIM = 64
SSD_HEADS = GROUP_WIDTH // SSD_HEAD_DIM
SSD_GROUPS = 2
SSD_STATE = 128
SSD_CONV = 4
SSD_CHUNK = 128
SSD_XBC = GROUP_WIDTH + 2 * SSD_GROUPS * SSD_STATE
SC_WIDTH = GROUP_WIDTH
SC_CONV = 3
D_FF = 2816
N_EXPERTS = 8
TOP_K = 2
D_FF_EXPERT = 3584
MOE_BLOCK = 256
EPS = 1e-6

QK_WIDTH = ATTN_HEADS * 2 * ATTN_HEAD_DIM
IN_WIDTHS = (QK_WIDTH, QK_WIDTH, ATTN_HEADS * 2 * ATTN_HEAD_DIM,
             GROUP_WIDTH, SSD_XBC, SSD_HEADS,
             SC_WIDTH, SC_WIDTH, SC_WIDTH)
IN_COLS = sum(IN_WIDTHS)
IN_SPLITS = tuple(int(v) for v in np.cumsum(IN_WIDTHS)[:-1])

kernel_name = 'hymba_style_diffattn_ssd_shortconv_moe'

def rms_norm(x, g):
    xf = x.astype(jnp.float32)
    y = xf * lax.rsqrt(jnp.mean(xf * xf, axis=-1, keepdims=True) + EPS)
    return (y * g.astype(jnp.float32)).astype(x.dtype)

def gated_group_rmsnorm(y, z, g, groups):
    v = y.astype(jnp.float32) * jax.nn.silu(z.astype(jnp.float32))
    shp = v.shape
    v = v.reshape(shp[:-1] + (groups, shp[-1] // groups))
    v = v * lax.rsqrt(jnp.mean(v * v, axis=-1, keepdims=True) + EPS)
    return v.reshape(shp) * g.astype(jnp.float32)

def causal_depthwise_conv(u, w):
    k, ch = w.shape
    return lax.conv_general_dilated(
        u, w[:, None, :].astype(u.dtype), window_strides=(1,), padding=((k - 1, 0),),
        dimension_numbers=('NWC', 'WIO', 'NWC'), feature_group_count=ch)

def diff_attention(q, k, v, lam):
    b, s, h, _, d = q.shape
    nq = s // Q_BLOCK
    qb = jnp.moveaxis(q.reshape(b, nq, Q_BLOCK, h, 2, d), 1, 0)
    key_pos = jnp.arange(s)
    scale = d ** -0.5

    def block(args):
        q_blk, blk_idx = args
        scores = jnp.einsum('bqhmd,bkhmd->bhmqk', q_blk, k).astype(jnp.float32) * scale
        q_pos = blk_idx * Q_BLOCK + jnp.arange(Q_BLOCK)
        causal = key_pos[None, :] <= q_pos[:, None]
        p = jax.nn.softmax(jnp.where(causal, scores, -jnp.inf), axis=-1)
        p_diff = p[:, :, 0] - lam * p[:, :, 1]
        return jnp.einsum('bhqk,bkhe->bqhe', p_diff.astype(v.dtype), v)

    out = lax.map(block, (qb, jnp.arange(nq)))
    return jnp.moveaxis(out, 0, 1).reshape(b, s, h, 2 * d)

def ssd_chunked_scan(xh, dt, a, bm, cm):
    b, s, h, p = xh.shape
    g, n = bm.shape[2], bm.shape[3]
    r = h // g
    L = SSD_CHUNK
    nc = s // L
    x = xh.reshape(b, nc, L, g, r, p)
    dt = dt.reshape(b, nc, L, g, r)
    bm = bm.reshape(b, nc, L, g, n)
    cm = cm.reshape(b, nc, L, g, n)
    a_cum = jnp.cumsum(dt * a.reshape(g, r), axis=2)
    xdt = x * dt[..., None]
    causal = jnp.tril(jnp.ones((L, L), dtype=bool))[:, :, None, None]
    seg = a_cum[:, :, :, None] - a_cum[:, :, None, :]
    decay = jnp.exp(jnp.where(causal, seg, -jnp.inf))
    cb = jnp.einsum('bclgn,bcsgn->bclsg', cm, bm)
    y_diag = jnp.einsum('bclsgr,bcsgrp->bclgrp', decay * cb[..., None], xdt)
    decay_to_end = jnp.exp(a_cum[:, :, -1:] - a_cum)
    states = jnp.einsum('bclgn,bclgrp->bcgrpn', bm, xdt * decay_to_end[..., None])
    chunk_decay = jnp.exp(a_cum[:, :, -1])

    def step(carry, inp):
        st, dec = inp
        return carry * dec[..., None, None] + st, carry

    init = jnp.zeros((b, g, r, p, n), xh.dtype)
    _, prev = lax.scan(step, init, (jnp.moveaxis(states, 1, 0), jnp.moveaxis(chunk_decay, 1, 0)))
    prev = jnp.moveaxis(prev, 0, 1)
    y_off = jnp.einsum('bclgn,bcgrpn->bclgrp', cm, prev) * jnp.exp(a_cum)[..., None]
    return (y_diag + y_off).reshape(b, s, h, p)

def hybrid_mixer(h, layer_idx, w_in, w_out, lambda_qk, attn_subln, conv_w, conv_b,
                 dt_bias, a_log, d_skip, ssd_norm_g, sconv_w):
    b, s, _ = h.shape
    f32 = jnp.float32
    q, k, v, z, xbc, dt, gate_b, gate_c, u = jnp.split(h @ w_in, IN_SPLITS, axis=-1)
    q = q.reshape(b, s, ATTN_HEADS, 2, ATTN_HEAD_DIM)
    k = k.reshape(b, s, ATTN_HEADS, 2, ATTN_HEAD_DIM)
    v = v.reshape(b, s, ATTN_HEADS, 2 * ATTN_HEAD_DIM)
    lam_init = 0.8 - 0.6 * math.exp(-0.3 * layer_idx)
    lq = lambda_qk.astype(f32)
    lam = jnp.exp(jnp.sum(lq[0] * lq[1])) - jnp.exp(jnp.sum(lq[2] * lq[3])) + lam_init
    attn = diff_attention(q, k, v, lam)
    attn = (rms_norm(attn, attn_subln) * (1.0 - lam_init)).reshape(b, s, GROUP_WIDTH)
    xbc = jax.nn.silu(causal_depthwise_conv(xbc, conv_w) + conv_b)
    xs, bm, cm = jnp.split(xbc, (GROUP_WIDTH, GROUP_WIDTH + SSD_GROUPS * SSD_STATE), axis=-1)
    dt = jax.nn.softplus(dt.astype(f32) + dt_bias.astype(f32))
    a = -jnp.exp(a_log.astype(f32))
    xh = xs.reshape(b, s, SSD_HEADS, SSD_HEAD_DIM).astype(f32)
    ys = ssd_chunked_scan(xh, dt, a,
                          bm.reshape(b, s, SSD_GROUPS, SSD_STATE).astype(f32),
                          cm.reshape(b, s, SSD_GROUPS, SSD_STATE).astype(f32))
    ys = (ys + d_skip.astype(f32)[:, None] * xh).reshape(b, s, GROUP_WIDTH)
    ssd = gated_group_rmsnorm(ys, z, ssd_norm_g, SSD_GROUPS).astype(h.dtype)
    sconv = gate_b * causal_depthwise_conv(gate_c * u, sconv_w)
    return jnp.concatenate([attn, ssd, sconv], axis=-1) @ w_out

def swiglu(h, w1, w3, w2):
    return (jax.nn.silu(h @ w1) * (h @ w3)) @ w2

def moe_swiglu(h, w_router, w1, w3, w2):
    b, s, d = h.shape
    xt = h.reshape(-1, d)
    n = xt.shape[0]
    logits = (xt @ w_router).astype(jnp.float32)
    top_logits, top_idx = lax.top_k(logits, TOP_K)
    gates = jax.nn.softmax(top_logits, axis=-1)
    n_assign = n * TOP_K
    e_flat = top_idx.reshape(-1)
    g_flat = gates.reshape(-1)
    t_flat = jnp.repeat(jnp.arange(n, dtype=jnp.int32), TOP_K)
    order = jnp.argsort(e_flat)
    e_sorted, t_sorted, g_sorted = e_flat[order], t_flat[order], g_flat[order]
    counts = jnp.bincount(e_flat, length=N_EXPERTS)
    padded = (counts + MOE_BLOCK - 1) // MOE_BLOCK * MOE_BLOCK
    start = jnp.cumsum(counts) - counts
    pstart = jnp.cumsum(padded) - padded
    dest = pstart[e_sorted] + jnp.arange(n_assign) - start[e_sorted]
    p_len = -(-n_assign // MOE_BLOCK) * MOE_BLOCK + N_EXPERTS * MOE_BLOCK
    n_blocks = p_len // MOE_BLOCK
    tok_buf = jnp.zeros((p_len,), jnp.int32).at[dest].set(t_sorted)
    gate_buf = jnp.zeros((p_len,), jnp.float32).at[dest].set(g_sorted)
    block_expert = jnp.minimum(
        jnp.searchsorted(jnp.cumsum(padded), jnp.arange(n_blocks) * MOE_BLOCK, side='right'),
        N_EXPERTS - 1)
    xb = xt[tok_buf].reshape(n_blocks, MOE_BLOCK, d)

    def expert_block(args):
        x_blk, e = args
        return swiglu(x_blk, w1[e], w3[e], w2[e])

    yb = lax.map(expert_block, (xb, block_expert)).reshape(p_len, d)
    y = jax.ops.segment_sum(yb * gate_buf[:, None].astype(yb.dtype), tok_buf, num_segments=n)
    return y.reshape(b, s, d)

def setup_inputs(seed: int = 0) -> dict:
    key = jax.random.key(seed)
    ks = jax.random.split(key, 26)
    f32 = jnp.float32
    n_dense = (DEPTH + 1) // 2
    n_moe = DEPTH // 2

    def nrm(i, shape, scale):
        return jax.random.normal(ks[i], shape, f32) * scale

    def gain(i, shape):
        return 1.0 + 0.05 * jax.random.normal(ks[i], shape, f32)

    dt0 = jnp.exp(jax.random.uniform(ks[14], (DEPTH, SSD_HEADS), f32, math.log(1e-3), math.log(1e-1)))
    return {
        'x': nrm(0, (BATCH, SEQ, D_MODEL), 1.0),
        'c': nrm(1, (BATCH, D_MODEL), 1.0),
        'w_mod': nrm(2, (DEPTH, D_MODEL, 6 * D_MODEL), D_MODEL ** -0.5),
        'b_mod': nrm(3, (DEPTH, 6 * D_MODEL), 0.02),
        'norm_mix_pre': gain(4, (DEPTH, D_MODEL)),
        'norm_mix_post': gain(5, (DEPTH, D_MODEL)),
        'norm_ffn_pre': gain(6, (DEPTH, D_MODEL)),
        'norm_ffn_post': gain(7, (DEPTH, D_MODEL)),
        'w_in': nrm(8, (DEPTH, D_MODEL, IN_COLS), D_MODEL ** -0.5),
        'w_out': nrm(9, (DEPTH, D_MIX, D_MODEL), D_MIX ** -0.5),
        'lambda_qk': nrm(10, (DEPTH, 4, ATTN_HEAD_DIM), 0.1),
        'attn_subln': gain(11, (DEPTH, 2 * ATTN_HEAD_DIM)),
        'ssd_conv_w': nrm(12, (DEPTH, SSD_CONV, SSD_XBC), SSD_CONV ** -0.5),
        'ssd_conv_b': nrm(13, (DEPTH, SSD_XBC), 0.02),
        'ssd_dt_bias': dt0 + jnp.log(-jnp.expm1(-dt0)),
        'ssd_a_log': jnp.log(jax.random.uniform(ks[15], (DEPTH, SSD_HEADS), f32, 1.0, 16.0)),
        'ssd_d': gain(16, (DEPTH, SSD_HEADS)),
        'ssd_norm': gain(17, (DEPTH, GROUP_WIDTH)),
        'sconv_w': nrm(18, (DEPTH, SC_CONV, SC_WIDTH), SC_CONV ** -0.5),
        'ffn_w1': nrm(19, (n_dense, D_MODEL, D_FF), D_MODEL ** -0.5),
        'ffn_w3': nrm(20, (n_dense, D_MODEL, D_FF), D_MODEL ** -0.5),
        'ffn_w2': nrm(21, (n_dense, D_FF, D_MODEL), D_FF ** -0.5),
        'moe_router': nrm(22, (n_moe, D_MODEL, N_EXPERTS), D_MODEL ** -0.5),
        'moe_w1': nrm(23, (n_moe, N_EXPERTS, D_MODEL, D_FF_EXPERT), D_MODEL ** -0.5),
        'moe_w3': nrm(24, (n_moe, N_EXPERTS, D_MODEL, D_FF_EXPERT), D_MODEL ** -0.5),
        'moe_w2': nrm(25, (n_moe, N_EXPERTS, D_FF_EXPERT, D_MODEL), D_FF_EXPERT ** -0.5),
    }

def reference(x, c, w_mod, b_mod, norm_mix_pre, norm_mix_post, norm_ffn_pre, norm_ffn_post,
              w_in, w_out, lambda_qk, attn_subln, ssd_conv_w, ssd_conv_b, ssd_dt_bias,
              ssd_a_log, ssd_d, ssd_norm, sconv_w, ffn_w1, ffn_w3, ffn_w2,
              moe_router, moe_w1, moe_w3, moe_w2):
    c_act = jax.nn.silu(c)
    for i in range(DEPTH):
        mod = c_act @ w_mod[i] + b_mod[i]
        shift_m, scale_m, gate_m, shift_f, scale_f, gate_f = [m[:, None, :] for m in jnp.split(mod, 6, axis=-1)]
        h = rms_norm(x, norm_mix_pre[i]) * (1.0 + scale_m) + shift_m
        y = hybrid_mixer(h, i, w_in[i], w_out[i], lambda_qk[i], attn_subln[i],
                         ssd_conv_w[i], ssd_conv_b[i], ssd_dt_bias[i], ssd_a_log[i],
                         ssd_d[i], ssd_norm[i], sconv_w[i])
        x = x + gate_m * rms_norm(y, norm_mix_post[i])
        h = rms_norm(x, norm_ffn_pre[i]) * (1.0 + scale_f) + shift_f
        if i % 2 == 0:
            y = swiglu(h, ffn_w1[i // 2], ffn_w3[i // 2], ffn_w2[i // 2])
        else:
            y = moe_swiglu(h, moe_router[i // 2], moe_w1[i // 2], moe_w3[i // 2], moe_w2[i // 2])
        x = x + gate_f * rms_norm(y, norm_ffn_post[i])
    return x


_drawn_inputs = setup_inputs


def setup_inputs(seed=0):
    import zlib

    import numpy as np

    out = dict(_drawn_inputs(seed))
    spreads = {}
    factors = {'lambda_qk': 2.695,
     'ssd_conv_b': 3.078,
     'ssd_d': 18.791,
     'attn_subln': 3.187,
     'ssd_norm': 2.946}
    for name, (base, spread) in spreads.items():
        noise = np.random.default_rng([zlib.crc32(name.encode()), seed]).standard_normal(out[name].shape)
        drawn = base * np.exp(spread * noise) if base else spread * noise
        out[name] = jnp.asarray(drawn.astype(out[name].dtype))
    for name, factor in factors.items():
        out[name] = (out[name] * factor).astype(out[name].dtype)
    return out
```

```python
import math
from contextlib import ExitStack

import concourse.bass as bass
from concourse import mybir

ALU = mybir.AluOpType
ACT = mybir.ActivationFunctionType
AX = mybir.AxisListType
F32 = mybir.dt.float32
I32 = mybir.dt.int32
U32 = mybir.dt.uint32

P = 128
EPS = 1e-6
NEG = -1e30

D = 1024
SEQ = 256
DEPTH = 2
GW = D // 2
HEADS = 4
HD = GW // (2 * HEADS)
SH, SP_, SG, SN = 8, 64, 2, 128
XBC = GW + 2 * SG * SN
SCONV, CCONV = 3, 4
FF = 2816
NE = 8
FE = 3584
KT = D // P
TT = SEQ // P
NM = 6 * KT

OFF = dict(q=0, k=GW, v=2 * GW, z=3 * GW, xbc=4 * GW, dt=4 * GW + XBC)
OFF["gb"] = OFF["dt"] + SH
OFF["gc"] = OFF["gb"] + GW
OFF["u"] = OFF["gc"] + GW

SLOT = 2048
RING = 7
FCH = 512
NCH = FE // FCH
JOB_SLOTS = NCH * 6
EXTRA = 3
NJOB = NE + EXTRA

OUTS = [("xbc", 0), ("xbc", 1), ("xbc", 2), ("xbc", 3), ("q", 0), ("q", 1), ("k", 0), ("k", 1),
        ("v", 0), ("v", 1), ("gc", 0), ("gc", 1), ("u", 0), ("u", 1), ("z", 0), ("z", 1),
        ("gb", 0), ("gb", 1)]
NOUT = len(OUTS)
TOKEN_MAJOR = ("v", "z")

STEPS = []
_AFTER = {
    0: [("conv", 0)], 1: [("conv", 1)], 2: [("conv", 2)], 3: [("dt", 0), ("conv", 3)],
    5: [("cum", 0)], 7: [("tok", 0)],
    9: [("decay", 0), ("soft", 0)],
    10: [("soft", 1), ("pt", 0)],
    11: [("ssd", 0), ("pv", 0), ("soft", 2), ("pt", 1)],
    12: [("decay", 1), ("pv", 1), ("soft", 3), ("pt", 2)],
    13: [("ssd", 1), ("pv", 2), ("soft", 4), ("pt", 3)],
    14: [("pv", 3), ("soft", 5), ("pt", 4)],
    15: [("ssdnorm", 0), ("pv", 4), ("soft", 6), ("pt", 5)],
    16: [("pv", 5), ("soft", 7), ("pt", 6)],
    17: [("sconv", 0), ("pv", 6), ("ssdT", 0), ("pt", 7), ("pv", 7), ("attn", 0)],
}
for _i in range(NOUT):
    STEPS.append(("out", _i))
    STEPS += _AFTER.get(_i, [])
NU = HEADS * TT

RMS = ["pre_mix", "ssd", "attn", "post_mix", "pre_ffn", "post_ffn"]
RMS_OF = dict(pre_mix=D, ssd=GW // SG, attn=2 * HD, post_mix=D, pre_ffn=D, post_ffn=D)


def lam_init(layer):
    return 0.8 - 0.6 * math.exp(-0.3 * layer)


def build(nc, x, c, w_mod, b_mod, norm_mix_pre, norm_mix_post, norm_ffn_pre, norm_ffn_post,
          w_in, w_out, lambda_qk, attn_subln, ssd_conv_w, ssd_conv_b, ssd_dt_bias,
          ssd_a_log, ssd_d, ssd_norm, sconv_w, ffn_w1, ffn_w3, ffn_w2,
          moe_router, moe_w1, moe_w3, moe_w2, out):

    def k_rows(w, k0, nk, col, n):
        return w.rearrange("(t p) n -> p t n", p=P)[:, k0:k0 + nk, col:col + n]

    def mod_entries(l):
        return [(("mod", l, i), k_rows(w_mod[l], 0, KT, i * 256, 256)) for i in range(NM // 2)]

    def mixer_entries(l):
        e = []
        for kind, half in OUTS:
            if kind in TOKEN_MAJOR:
                e.append(((kind, l, half), k_rows(w_in[l], half * 4, 4, OFF[kind], 512)))
            else:
                e.append(((kind, l, half), k_rows(w_in[l], 0, KT, OFF[kind] + 256 * half, 256)))
        e += [(("wout", l, r), k_rows(w_out[l], 2 * r, 2, 0, D)) for r in WOUT_ORDER]
        return e

    WOUT_ORDER = [4, 5, 2, 3, 0, 1]
    NQ = FF // 256

    def ffn_entries():
        w1, w3, w2 = ffn_w1[0], ffn_w3[0], ffn_w2[0]
        e = []
        for q in range(NQ + 1):
            if q < NQ:
                e.append((("f1", q), k_rows(w1, 0, KT, q * 256, 256)))
                e.append((("f3", q), k_rows(w3, 0, KT, q * 256, 256)))
            if q:
                e.append((("f2", q - 1), k_rows(w2, 2 * (q - 1), 2, 0, D)))
        return e

    stream = mod_entries(0) + mixer_entries(0) + ffn_entries() + mod_entries(1) + mixer_entries(1)
    NS = len(stream)

    def job_order():
        o = []
        for ch in range(NCH + 1):
            if ch < NCH:
                o += [("w1", ch, 0), ("w1", ch, 1), ("w3", ch, 0), ("w3", ch, 1)]
            if ch:
                o += [("w2", ch - 1, 0), ("w2", ch - 1, 1)]
        return o

    JOB = job_order()
    assert len(JOB) == JOB_SLOTS and JOB_SLOTS % RING == 0
    w1_v = moe_w1[0].rearrange("e (t p) n -> e p t n", p=P)
    w3_v = moe_w3[0].rearrange("e (t p) n -> e p t n", p=P)
    w2_v = moe_w2[0].rearrange("e (t p) n -> e p t n", p=P)

    def job_source(e, kind, ch, half):
        if kind == "w2":
            return w2_v[bass.ds(e, 1), :, ch * 4 + half * 2:ch * 4 + half * 2 + 2, :].rearrange("e p t n -> (e p) t n")
        v = w1_v if kind == "w1" else w3_v
        return v[bass.ds(e, 1), :, half * 4:half * 4 + 4, ch * FCH:(ch + 1) * FCH].rearrange("e p t n -> (e p) t n")

    with ExitStack() as ctx:
        def sb(name, shape, dt=F32):
            return ctx.enter_context(nc.sbuf_tensor(name, shape, dt))

        def sem(name):
            return ctx.enter_context(nc.semaphore(name))

        ring = sb("weight_ring", [P, RING, SLOT])
        x_tok = sb("x_tok", [P, TT, D])
        xn = sb("xn", [P, TT, D])
        hT = sb("hT", [P, KT, SEQ])
        praw = sb("praw", [P, 3, P])
        pcol = sb("pcol", [P, 3 * P])
        gate_row = sb("gate_row", [P, 2, D])
        modc = sb("modc", [P, DEPTH, NM])
        acol = sb("acol", [P, DEPTH, 2, KT])
        gcol = sb("gcol", [P, DEPTH, 2, KT])
        subc = sb("subc", [P, DEPTH])
        c_act = sb("c_act", [P, KT])
        ident = sb("ident", [P, P])
        ones = sb("ones", [P, P])
        upper = sb("upper", [P, P])
        strict = sb("strict", [P, P])
        maskT = sb("maskT", [P, P])
        maskq = sb("maskq", [P, 2, P])
        iota = sb("iota", [P, P])
        neghalf = sb("neghalf", [P, 8])
        small = sb("small", [P, 3, DEPTH * SH])
        lamq = sb("lamq", [P, DEPTH, 4, HD])
        lamp = sb("lamp", [P, DEPTH, 2, HD])
        lams = sb("lams", [P, DEPTH, 2])
        lame = sb("lame", [P, DEPTH, 2])
        nlam = sb("nlam", [P, DEPTH])
        aexp = sb("aexp", [P, DEPTH * SH])
        wdt = sb("wdt", [P, DEPTH, KT, SH])
        wrt = sb("wrt", [P, KT, NE])
        sumsq = sb("sumsq", [P, DEPTH * len(RMS), 8])
        msq = sb("msq", [P, DEPTH * len(RMS), 8])
        rstd = sb("rstd", [P, DEPTH * len(RMS), 8])
        square = sb("square", [P, D])
        tmpx = xn

        ARENA = 25088
        arena = sb("arena", [P, ARENA])
        at = [0]

        def carve(*shape):
            n = math.prod(shape)
            a = arena[:, at[0]:at[0] + n]
            at[0] += n
            assert at[0] <= ARENA, at[0]
            if len(shape) == 1:
                return a
            names = "abcd"[:len(shape)]
            return a.rearrange(f"p ({' '.join(names)}) -> p {' '.join(names)}",
                               **{k: v for k, v in zip(names[1:], shape[1:])})

        PADX = CCONV - 1
        PADU = SCONV - 1
        xbcT = carve(8, PADX + SEQ)
        cacc = carve(2, SEQ)
        convT = carve(8, SEQ)
        qT = carve(HEADS, SEQ)
        kT = carve(HEADS, SEQ)
        v_tok = carve(TT, GW)
        sz = carve(TT, GW)
        gcT = carve(4, SEQ)
        uT = carve(4, PADU + SEQ)
        gbT = carve(4, SEQ)
        mixT = carve(12, SEQ)
        xs_tok = carve(TT, GW)
        xdt = carve(TT, GW)
        xdte = carve(GW)
        b_tok = carve(SG, SN)
        decay = carve(SH, P)
        prev = carve(GW)
        ytok = carve(TT, GW)
        s_sb = carve(2, 2, SEQ)
        e_sb = carve(2, 2, SEQ)
        pd = carve(2, SEQ)
        ptT = carve(2, SEQ)
        o_tok = carve(TT, GW)
        dtr = carve(TT, SH)
        dta = carve(TT, SH)
        dte_ = carve(TT, SH)
        dtu = carve(TT, SH)
        dtl = carve(TT, SH)
        dtz = carve(TT, SH)
        dtv = carve(TT, SH)
        dA = carve(TT, SH)
        acum = carve(TT, SH)
        dsub = carve(SH)
        dend = carve(SH)
        eacum = carve(SH)
        mx = carve(2, 2)
        nb = carve(2, 2)
        es = carve(2, 2)
        er = carve(2, 2)
        at[0] = 0
        f_silu = carve(2, 2, SEQ)
        f_act = carve(2, 2, SEQ)
        at[0] = 0
        y_moe = carve(TT, D)
        xeT = carve(KT, P)
        m_silu = carve(FCH)
        m_act = carve(2, FCH)
        m_actT = carve(2, 4, P)
        y_e = carve(D)
        sel = carve(TT, P)
        selg = carve(TT, P)
        selgT = carve(TT, P)
        lg = carve(TT, NE)
        lmx = carve(TT, NE)
        lixf = carve(TT, 2)
        oh1 = carve(TT, NE)
        oh2 = carve(TT, NE)
        msk = carve(TT, NE)
        gts = carve(TT, NE)
        ldel = carve(TT)
        led = carve(TT)
        lden = carve(TT)
        lg1 = carve(TT)
        lg2 = carve(TT)
        posj = carve(TT, NJOB)
        mskj = carve(TT, NJOB)
        gtsj = carve(TT, NJOB)
        cnts = carve(NE)
        over = carve(NE)
        ranki = carve(NE)
        rank = carve(NE)
        ohk = carve(EXTRA, NE)
        pick = carve(TT, EXTRA, NE)
        epick = carve(EXTRA, NE)
        ejobf = carve(NJOB)
        njf = carve(1)
        lix = sb("lix", [P, TT, NE], U32)
        ejob = sb("ejob", [P, NJOB], I32)
        njob = sb("njob", [P, 1], I32)

        ps = ctx.enter_context(nc.psum_tensor("ps", [P, 8, 512], F32))

        def pair(b):
            return ps[:, b:b + 2, :].rearrange("p b n -> p (b n)")

        landed = [sem(f"weights_landed{i}") for i in range(RING)]
        w_used = sem("w_used")
        x_landed = sem("x_landed")
        par_landed = sem("par_landed")
        consts = sem("consts")
        zeroed = sem("zeroed")
        parT = sem("parT")
        pars = sem("pars")
        c_ready = sem("c_ready")
        lam_s = sem("lam_s")
        lam_e = sem("lam_e")
        mod_done = sem("mod_done")
        mod_ready = sem("mod_ready")
        grow_done = sem("grow_done")
        grow_ready = sem("grow_ready")
        ss_ready = sem("ss_ready")
        rstd_ready = sem("rstd_ready")
        xn_ready = sem("xn_ready")
        xnT_ready = sem("xnT_ready")
        hT_ready = sem("hT_ready")
        proj_done = sem("proj_done")
        proj_out = sem("proj_out")
        conv_acc = sem("conv_acc")
        conv_done = sem("conv_done")
        dt_mm = sem("dt_mm")
        dt_a = sem("dt_a")
        dt_e = sem("dt_e")
        dt_ready = sem("dt_ready")
        cum_done = sem("cum_done")
        cum_sub = sem("cum_sub")
        cum_exp = sem("cum_exp")
        tok_done = sem("tok_done")
        tok_dve = sem("tok_dve")
        tok_act = sem("tok_act")
        row_done = sem("row_done")
        seg_ready = sem("seg_ready")
        dec_ready = sem("dec_ready")
        mt_ready = sem("mt_ready")
        y_done = sem("y_done")
        y_out = sem("y_out")
        st_ready = sem("st_ready")
        v_ready = sem("v_ready")
        vn_ready = sem("vn_ready")
        ssdT = sem("ssdT")
        ssd_mix = sem("ssd_mix")
        sc_mix = sem("sc_mix")
        sc_done = sem("sc_done")
        sm_ready = sem("sm_ready")
        e_ready = sem("e_ready")
        pd_ready = sem("pd_ready")
        pt_done = sem("pt_done")
        pt_ready = sem("pt_ready")
        pv_done = sem("pv_done")
        pv_out = sem("pv_out")
        on_ready = sem("on_ready")
        attT = sem("attT")
        att_mix = sem("att_mix")
        ysub_done = sem("ysub_done")
        x_ready = sem("x_ready")
        f_up = sem("f_up")
        f_sl = sem("f_sl")
        f_ac = sem("f_ac")
        f_dn = sem("f_dn")
        htok_done = sem("htok_done")
        htok_out = sem("htok_out")
        lg_done = sem("lg_done")
        r_del = sem("r_del")
        r_exp = sem("r_exp")
        pos_done = sem("pos_done")
        routed = sem("routed")
        sel_ready = sem("sel_ready")
        gat_done = sem("gat_done")
        gat_out = sem("gat_out")
        m_up = sem("m_up")
        m_sl = sem("m_sl")
        m_ac = sem("m_ac")
        m_tp = sem("m_tp")
        m_tc = sem("m_tc")
        m_dn = sem("m_dn")
        ye_out = sem("ye_out")
        sca_done = sem("sca_done")
        sca_out = sem("sca_out")
        stored = sem("stored")

        block = ctx.enter_context(nc.Block())

        def rq(l, name):
            return l * len(RMS) + RMS.index(name)

        def col(tile, row):
            return pcol[:, tile * P + row:tile * P + row + 1]

        def cols(tile, row, n):
            return pcol[:, tile * P + row:tile * P + row + n]

        ROW_BMOD = 8
        GAIN = {"pre_mix": 0, "post_mix": 16, "pre_ffn": 32, "post_ffn": 48}
        ROW_CW = 64
        ROW_CB, ROW_SW, ROW_SN, ROW_AS = 0, 16, 40, 48
        DT_BIAS, A_LOG, D_SKIP = range(3)

        DTC, ACC, ALC, CBC = 0, 16, 32, 256

        @block.sync
        def _(sp):
            sp.dma_start(x_tok[:], x.rearrange("b (t p) d -> p (b t) d", p=P)).then_inc(x_landed, 16)
            for n, (tag, src) in enumerate(stream):
                if n >= RING:
                    sp.wait_ge(w_used, n - RING + 1)
                sp.dma_start(ring[:, n % RING, :].rearrange("p (a b) -> p a b", a=src.shape[1]),
                             src).then_inc(landed[n % RING], 16)

            def load_expert(job, e):
                for i, (kind, ch, half) in enumerate(JOB):
                    s = (NS + i) % RING
                    sp.wait_ge(w_used, job * JOB_SLOTS + (NS + i - RING + 1))
                    src = job_source(e, kind, ch, half)
                    sp.dma_start(ring[:, s, :].rearrange("p (a b) -> p a b", a=src.shape[1]),
                                 src).then_inc(landed[s], 16)

            with sp.Fori(0, NE) as e:
                load_expert(e, e)
            sp.wait_ge(routed, 1)
            n_jobs = sp.value_load(njob[0:1, 0:1], min_val=NE, max_val=NJOB)
            with sp.If(n_jobs > NE):
                with sp.Fori(NE, n_jobs) as job:
                    e = sp.value_load(ejob[0:1, bass.ds(job, 1)], min_val=0, max_val=NE - 1)
                    load_expert(job, e)
            sp.wait_ge(x_ready, 2 * DEPTH)
            sp.dma_start(out.rearrange("b (t p) d -> p (b t) d", p=P), x_tok[:]).then_inc(stored, 16)
            sp.wait_ge(stored, 16)

        @block.gpsimd
        def _(pool):
            nc.gpsimd.memset(ones[:], 1.0)
            nc.gpsimd.memset(neghalf[:], -0.5)
            nc.gpsimd.memset(maskq[:], 0.0)
            nc.gpsimd.memset(maskT[:], 0.0)
            nc.gpsimd.memset(ident[:], 0.0)
            nc.gpsimd.drain()
            nc.gpsimd.affine_select(out=ident[:], in_=ident[:], compare_op=ALU.not_equal, fill=1.0,
                                    base=0, pattern=[[-1, P]], channel_multiplier=1)
            nc.gpsimd.affine_select(out=upper[:], in_=ones[:], compare_op=ALU.is_ge, fill=0.0,
                                    base=0, pattern=[[1, P]], channel_multiplier=-1)
            nc.gpsimd.affine_select(out=strict[:], in_=ones[:], compare_op=ALU.is_gt, fill=0.0,
                                    base=0, pattern=[[1, P]], channel_multiplier=-1)
            nc.gpsimd.affine_select(out=maskT[:], in_=maskT[:], compare_op=ALU.is_ge, fill=NEG,
                                    base=0, pattern=[[1, P]], channel_multiplier=-1)
            nc.gpsimd.affine_select(out=maskq[:, 1, :], in_=maskq[:, 1, :], compare_op=ALU.is_ge, fill=NEG,
                                    base=0, pattern=[[-1, P]], channel_multiplier=1)
            nc.gpsimd.iota(iota[:], pattern=[[1, P]], base=0, channel_multiplier=0,
                           allow_small_or_imprecise_dtypes=True)
            nc.gpsimd.drain().then_inc(consts, 1)

            def serve_rms(l, name, n):
                r = rq(l, name)
                pool.wait_ge(ss_ready, r + 1)
                nc.gpsimd.tensor_scalar(msq[:, r, 0:n], sumsq[:, r, 0:n], 1.0 / RMS_OF[name], EPS, ALU.mult, ALU.add)
                nc.gpsimd.drain()
                nc.gpsimd.tensor_tensor(rstd[:, r, 0:n], msq[:, r, 0:n], neghalf[:, 0:n],
                                        ALU.pow).then_inc(rstd_ready, 1)

            for l in range(DEPTH):
                serve_rms(l, "pre_mix", TT)
                for step, i in STEPS:
                    if step == "ssdnorm":
                        serve_rms(l, "ssd", TT * SG)
                    if step == "sconv":
                        pool.wait_ge(proj_out, NOUT * l + NOUT)
                        nc.gpsimd.memset(uT[:, :, 0:PADU], 0.0)
                        nc.gpsimd.tensor_tensor(uT[:, :, PADU:], uT[:, :, PADU:], gcT, ALU.mult)
                        nc.gpsimd.drain()
                        for j in range(4):
                            nc.gpsimd.tensor_scalar(mixT[:, 8 + j, :], uT[:, j, 0:SEQ],
                                                    col(2, ROW_SW + 12 * l + j), None, ALU.mult)
                        for k in range(1, SCONV):
                            for j in range(4):
                                nc.gpsimd.tensor_scalar(gcT[:, j, :], uT[:, j, k:k + SEQ],
                                                        col(2, ROW_SW + 12 * l + 4 * k + j), None, ALU.mult)
                            nc.gpsimd.drain()
                            nc.gpsimd.tensor_tensor(mixT[:, 8:12, :], mixT[:, 8:12, :], gcT, ALU.add)
                            nc.gpsimd.drain()
                        nc.gpsimd.tensor_tensor(mixT[:, 8:12, :], mixT[:, 8:12, :], gbT, ALU.mult)
                        nc.gpsimd.drain().then_inc(sc_mix, 1)
                    if step == "attn":
                        serve_rms(l, "attn", TT * HEADS)
                serve_rms(l, "post_mix", TT)
                serve_rms(l, "pre_ffn", TT)
                serve_rms(l, "post_ffn", TT)

        @block.scalar
        def _(act):
            act.wait_ge(zeroed, 1)
            loads = [(0, 0, c.rearrange("b (t p) -> (b t) p", p=P)),
                     (0, ROW_BMOD, b_mod.rearrange("l (t p) -> (l t) p", p=P)),
                     (1, GAIN["pre_mix"], norm_mix_pre.rearrange("l (t p) -> (l t) p", p=P)),
                     (1, GAIN["post_mix"], norm_mix_post.rearrange("l (t p) -> (l t) p", p=P)),
                     (1, GAIN["pre_ffn"], norm_ffn_pre.rearrange("l (t p) -> (l t) p", p=P)),
                     (1, GAIN["post_ffn"], norm_ffn_post.rearrange("l (t p) -> (l t) p", p=P)),
                     (1, ROW_CW, ssd_conv_w.rearrange("l k (t p) -> (l k t) p", p=P)),
                     (2, ROW_CB, ssd_conv_b.rearrange("l (t p) -> (l t) p", p=P)),
                     (2, ROW_SW, sconv_w.rearrange("l k (t p) -> (l k t) p", p=P)),
                     (2, ROW_SN, ssd_norm.rearrange("l (t p) -> (l t) p", p=P)),
                     (2, ROW_AS, attn_subln)]
            for tile, row, src in loads:
                act.dma_start(praw[row:row + src.shape[0], tile, :], src).then_inc(par_landed, 16)
            for i, v in enumerate((ssd_dt_bias, ssd_a_log, ssd_d)):
                act.dma_start(small[:, i, :], v.rearrange("l h -> (l h)").partition_broadcast(P)).then_inc(par_landed, 16)
            act.dma_start(lamq[:].rearrange("p l f d -> p (l f d)"),
                          lambda_qk.rearrange("l f d -> (l f d)").partition_broadcast(P)).then_inc(par_landed, 16)
            for l in range(DEPTH):
                act.dma_start(wdt[:, l], k_rows(w_in[l], 0, KT, OFF["dt"], SH)).then_inc(par_landed, 16)
            act.dma_start(wrt[:], k_rows(moe_router[0], 0, KT, 0, NE)).then_inc(par_landed, 16)

            act.wait_ge(pars, 1)
            nc.scalar.activation(c_act[:], cols(0, 0, KT), ACT.Silu).then_inc(c_ready, 1)
            nc.scalar.activation(aexp[:], small[:, A_LOG, :], ACT.Exp)
            act.wait_ge(lam_s, 1)
            nc.scalar.activation(lame[:], lams[:], ACT.Exp).then_inc(lam_e, 1)

            def squares(l, name, parts):
                r = rq(l, name)
                for i, a in enumerate(parts):
                    nc.scalar.activation(square[:, 0:a.shape[-1]], a, ACT.Square, accum_out=sumsq[:, r, i:i + 1])
                    nc.scalar.drain()
                nc.scalar.drain().then_inc(ss_ready, 1)

            def pre_norm(n, name):
                l = n // 2
                if n == 0:
                    act.wait_ge(x_landed, 16)
                else:
                    act.wait_ge(x_ready, n)
                squares(l, name, [x_tok[:, t, :] for t in range(TT)])

            def copy_projection(l, i):
                kind, half = OUTS[i]
                act.wait_ge(proj_done, NOUT * l + i + 1)
                b = ps[:, i % 3, :]
                two = b.rearrange("p (j n) -> p j n", j=2)
                dst = {"xbc": lambda: xbcT[:, 2 * half:2 * half + 2, PADX:], "q": lambda: qT[:, 2 * half:2 * half + 2, :],
                       "k": lambda: kT[:, 2 * half:2 * half + 2, :], "gc": lambda: gcT[:, 2 * half:2 * half + 2, :],
                       "gb": lambda: gbT[:, 2 * half:2 * half + 2, :], "u": lambda: uT[:, 2 * half:2 * half + 2, PADU:],
                       "v": lambda: v_tok[:, half, :], "z": lambda: sz[:, half, :]}[kind]()
                if kind == "z":
                    nc.scalar.activation(dst, b, ACT.Silu).then_inc(proj_out, 1)
                else:
                    nc.scalar.copy(dst, b if kind == "v" else two).then_inc(proj_out, 1)

            def mixer_step(l, step, i):
                if step == "out":
                    copy_projection(l, i)
                elif step == "conv":
                    act.wait_ge(conv_acc, 4 * l + i + 1)
                    nc.scalar.activation(convT[:, 2 * i:2 * i + 2, :], cacc, ACT.Silu).then_inc(conv_done, 1)
                elif step == "dt":
                    act.wait_ge(dt_a, 2 * l + 1)
                    nc.scalar.activation(dte_, dta, ACT.Exp).then_inc(dt_e, 1)
                    act.wait_ge(dt_a, 2 * l + 2)
                    nc.scalar.activation(dtl, dtu, ACT.Ln).then_inc(dt_e, 1)
                elif step == "cum":
                    act.wait_ge(cum_sub, l + 1)
                    nc.scalar.activation(dend, dsub, ACT.Exp)
                    nc.scalar.activation(eacum, acum[:, 1, :], ACT.Exp)
                    nc.scalar.drain().then_inc(cum_exp, 1)
                elif step == "tok":
                    act.wait_ge(tok_done, l + 1)
                    nc.scalar.copy(xs_tok, ps[:, 4:6, :])
                    nc.scalar.copy(b_tok.rearrange("p g n -> p (g n)"), ps[:, 3, CBC:CBC + SG * SN])
                    nc.scalar.drain().then_inc(tok_act, 1)
                elif step == "decay":
                    act.wait_ge(seg_ready, 2 * l + i + 1)
                    nc.scalar.activation(decay, decay, ACT.Exp).then_inc(dec_ready, 1)
                elif step == "ssd":
                    if i == 0:
                        act.wait_ge(y_done, 2 * l + 1)
                        nc.scalar.copy(prev, ps[:, 5, :]).then_inc(st_ready, 1)
                elif step == "ssdnorm":
                    act.wait_ge(v_ready, l + 1)
                    squares(l, "ssd", [ytok[:, t, g * 256:(g + 1) * 256] for t in range(TT) for g in range(SG)])
                elif step == "soft":
                    n = P * (i % TT + 1)
                    act.wait_ge(sm_ready, NU * l + i + 1)
                    for m in range(2):
                        nc.scalar.activation(e_sb[:, i % 2, m, 0:n], s_sb[:, i % 2, m, 0:n], ACT.Exp,
                                             bias=nb[:, i % 2, m:m + 1], scale=HD ** -0.5,
                                             accum_out=es[:, i % 2, m:m + 1])
                    nc.scalar.drain().then_inc(e_ready, 1)
                elif step == "pt":
                    n = P * (i % TT + 1)
                    act.wait_ge(pt_done, NU * l + i + 1)
                    nc.scalar.copy(ptT[:, i % 2, 0:n], ps[:, 7, 0:n]).then_inc(pt_ready, 1)
                elif step == "pv":
                    h, t = i // TT, i % TT
                    r = rq(l, "attn")
                    act.wait_ge(pv_done, NU * l + i + 1)
                    o = ps[:, 7, 256:384]
                    nc.scalar.copy(o_tok[:, t, h * P:(h + 1) * P], o)
                    nc.scalar.activation(square[:, 0:P], o, ACT.Square,
                                         accum_out=sumsq[:, r, t * HEADS + h:t * HEADS + h + 1])
                    nc.scalar.drain().then_inc(pv_out, 1)
                elif step == "attn":
                    nc.scalar.drain().then_inc(ss_ready, 1)

            for l in range(DEPTH):
                for s in range(2):
                    b = 6 if s == 0 else 4
                    act.wait_ge(grow_done, 2 * l + s + 1)
                    nc.scalar.copy(gate_row[:, s, :], pair(b)).then_inc(grow_ready, 1)
                pre_norm(2 * l, "pre_mix")
                for step, i in STEPS:
                    mixer_step(l, step, i)
                act.wait_ge(ysub_done, 2 * l + 1)
                squares(l, "post_mix", [pair(2 * t) for t in range(TT)])
                pre_norm(2 * l + 1, "pre_ffn")
                if l == 0:
                    for q in range(NQ):
                        act.wait_ge(f_up, q + 1)
                        if q >= 2:
                            act.wait_ge(f_ac, q - 1)
                        b = 2 * (q % 2)
                        nc.scalar.activation(f_silu[:, q % 2], ps[:, b, :].rearrange("p (j n) -> p j n", j=2),
                                             ACT.Silu).then_inc(f_sl, 1)
                    act.wait_ge(ysub_done, 2)
                    squares(l, "post_ffn", [pair(4 + 2 * t) for t in range(TT)])

            for g in range(4):
                act.wait_ge(htok_done, g + 1)
                nc.scalar.copy(xn[:, g // 2, (g % 2) * 512:(g % 2 + 1) * 512], ps[:, 4 + g % 2, :]).then_inc(htok_out, 1)
            act.wait_ge(r_del, 1)
            nc.scalar.activation(led, ldel, ACT.Exp).then_inc(r_exp, 1)
            act.wait_ge(routed, 1)
            n_jobs = act.value_load(njob[0:1, 0:1], min_val=NE, max_val=NJOB)
            with act.Fori(0, n_jobs) as job:
                for g in range(2):
                    act.wait_ge(gat_done, job * 3 + (g + 1))
                    nc.scalar.copy(xeT[:, 4 * g:4 * g + 4, :],
                                   ps[:, 6 + g, :].rearrange("p (k n) -> p k n", k=4)).then_inc(gat_out, 1)
                act.wait_ge(gat_done, job * 3 + 3)
                nc.scalar.copy(selgT, ps[:, 7, 0:TT * P].rearrange("p (t n) -> p t n", t=TT)).then_inc(gat_out, 1)
                for ch in range(NCH + 1):
                    if ch < NCH:
                        act.wait_ge(m_up, job * NCH + (ch + 1))
                        if ch:
                            act.wait_ge(m_ac, job * NCH + ch)
                        nc.scalar.activation(m_silu, ps[:, 2 * (ch % 2), :], ACT.Silu).then_inc(m_sl, 1)
                    if ch:
                        act.wait_ge(m_tp, job * NCH + ch)
                        nc.scalar.copy(m_actT[:, (ch - 1) % 2],
                                       ps[:, 6, :].rearrange("p (k n) -> p k n", k=4)).then_inc(m_tc, 1)
                act.wait_ge(m_dn, job + 1)
                nc.scalar.copy(y_e, pair(4)).then_inc(ye_out, 1)
            act.wait_ge(ysub_done, 2 * DEPTH)
            squares(DEPTH - 1, "post_ffn", [y_moe[:, t, :] for t in range(TT)])

        @block.vector
        def _(dve):
            nc.vector.memset(praw[:], 0.0).then_inc(zeroed, 1)
            dve.wait_ge(parT, 1)
            nc.vector.tensor_copy(pcol[:], ps[:, 7, 0:3 * P])
            nc.vector.drain().then_inc(pars, 1)
            nc.vector.tensor_tensor(lamp[:], lamq[:, :, 0::2, :], lamq[:, :, 1::2, :], ALU.mult)
            nc.vector.drain()
            nc.vector.tensor_reduce(lams[:], lamp[:], AX.X, ALU.add).then_inc(lam_s, 1)
            dve.wait_ge(lam_e, 1)
            nc.vector.tensor_tensor(nlam[:], lame[:, :, 1], lame[:, :, 0], ALU.subtract)
            nc.vector.drain()
            for l in range(DEPTH):
                nc.vector.tensor_scalar(nlam[:, l:l + 1], nlam[:, l:l + 1], -lam_init(l), None, ALU.add)
                nc.vector.tensor_scalar(subc[:, l:l + 1], col(2, ROW_AS + l), 1.0 - lam_init(l), None, ALU.mult)
            nc.vector.drain()

            def modulation(l):
                dve.wait_ge(mod_done, l + 1)
                nc.vector.tensor_tensor(modc[:, l], ps[:, 3, 0:NM], cols(0, ROW_BMOD + NM * l, NM), ALU.add)
                nc.vector.drain()
                for s, (pre, post) in enumerate((("pre_mix", "post_mix"), ("pre_ffn", "post_ffn"))):
                    o = 3 * KT * s
                    nc.vector.scalar_tensor_tensor(out=acol[:, l, s], in0=modc[:, l, o + KT:o + 2 * KT], scalar=1.0,
                                                   in1=cols(1, GAIN[pre] + KT * l, KT), op0=ALU.add, op1=ALU.mult)
                    nc.vector.tensor_tensor(gcol[:, l, s], modc[:, l, o + 2 * KT:o + 3 * KT],
                                            cols(1, GAIN[post] + KT * l, KT), ALU.mult)
                nc.vector.drain().then_inc(mod_ready, 1)

            def pre_norm(n, name):
                l, s = n // 2, n % 2
                r = rq(l, name)
                dve.wait_ge(rstd_ready, r + 1)
                for t in range(TT):
                    nc.vector.tensor_scalar(xn[:, t, :], x_tok[:, t, :], rstd[:, r, t:t + 1], None, ALU.mult)
                nc.vector.drain().then_inc(xn_ready, 1)
                for g in range(4):
                    dve.wait_ge(xnT_ready, 4 * n + g + 1)
                    for j in range(2):
                        kt = 2 * g + j
                        nc.vector.tensor_scalar(hT[:, kt, :], ps[:, 4 + g % 2, j * SEQ:(j + 1) * SEQ],
                                                acol[:, l, s, kt:kt + 1], modc[:, l, 3 * KT * s + kt:3 * KT * s + kt + 1],
                                                ALU.mult, ALU.add)
                    nc.vector.drain().then_inc(hT_ready, 1)

            def post_norm(l, s, name, parts):
                r = rq(l, name)
                dve.wait_ge(rstd_ready, r + 1)
                dve.wait_ge(grow_ready, 2 * l + s + 1)
                for t in range(TT):
                    nc.vector.scalar_tensor_tensor(out=tmpx[:, t, :], in0=parts[t], scalar=rstd[:, r, t:t + 1],
                                                   in1=gate_row[:, s, :], op0=ALU.mult, op1=ALU.mult)
                nc.vector.drain()
                nc.vector.tensor_tensor(x_tok[:], x_tok[:], tmpx[:], ALU.add)
                nc.vector.drain().then_inc(x_ready, 1)

            def per_head(a):
                return a.unsqueeze(2).to_broadcast([P, SH, SP_])

            def heads(a):
                return a.rearrange("p (h n) -> p h n", h=SH)

            def mixer_step(l, step, i):
                if step == "conv":
                    dve.wait_ge(proj_out, NOUT * l + i + 1)
                    if i == 0:
                        nc.vector.memset(xbcT[:, :, 0:PADX], 0.0)
                        nc.vector.drain()
                    if 4 * l + i > 0:
                        dve.wait_ge(conv_done, 4 * l + i)
                    for k in range(CCONV):
                        for j in range(2):
                            ct = 2 * i + j
                            w = col(1, ROW_CW + 8 * CCONV * l + 8 * k + ct)
                            if k == 0:
                                nc.vector.tensor_scalar(cacc[:, j, :], xbcT[:, ct, 0:SEQ], w,
                                                        col(2, ROW_CB + 8 * l + ct), ALU.mult, ALU.add)
                            else:
                                nc.vector.scalar_tensor_tensor(out=cacc[:, j, :], in0=xbcT[:, ct, k:k + SEQ], scalar=w,
                                                               in1=cacc[:, j, :], op0=ALU.mult, op1=ALU.add)
                        nc.vector.drain()
                    nc.vector.drain().then_inc(conv_acc, 1)
                elif step == "dt":
                    dve.wait_ge(dt_mm, l + 1)
                    bias = small[:, DT_BIAS, SH * l:SH * (l + 1)].unsqueeze(1).to_broadcast([P, TT, SH])
                    nc.vector.tensor_tensor(dtr, ps[:, 3, DTC:DTC + TT * SH].rearrange("p (t h) -> p t h", t=TT),
                                            bias, ALU.add)
                    nc.vector.drain()
                    nc.vector.scalar_tensor_tensor(out=dta, in0=dtr, scalar=-1.0, in1=dtr, op0=ALU.mult, op1=ALU.min)
                    nc.vector.drain()
                    nc.vector.tensor_scalar(dtr, dtr, 0.0, None, ALU.max)
                    nc.vector.drain().then_inc(dt_a, 1)
                    dve.wait_ge(dt_e, 2 * l + 1)
                    nc.vector.tensor_scalar(dtu, dte_, 1.0, None, ALU.add)
                    nc.vector.drain().then_inc(dt_a, 1)
                    nc.vector.tensor_scalar(dtv, dtu, -1.0, None, ALU.add)
                    nc.vector.drain()
                    nc.vector.tensor_scalar(dtz, dtv, 0.0, None, ALU.is_equal)
                    nc.vector.drain()
                    nc.vector.tensor_tensor(dtv, dtv, dtz, ALU.add)
                    nc.vector.drain()
                    nc.vector.reciprocal(dtv, dtv)
                    nc.vector.drain()
                    nc.vector.tensor_tensor(dtv, dtv, dte_, ALU.mult)
                    nc.vector.tensor_tensor(dtz, dtz, dte_, ALU.mult)
                    dve.wait_ge(dt_e, 2 * l + 2)
                    nc.vector.drain()
                    nc.vector.tensor_tensor(dtv, dtv, dtl, ALU.mult)
                    nc.vector.tensor_tensor(dtr, dtr, dtz, ALU.add)
                    nc.vector.drain()
                    nc.vector.tensor_tensor(dtr, dtr, dtv, ALU.add)
                    nc.vector.drain()
                    an = aexp[:, SH * l:SH * (l + 1)].unsqueeze(1).to_broadcast([P, TT, SH])
                    nc.vector.scalar_tensor_tensor(out=dA, in0=dtr, scalar=-1.0, in1=an, op0=ALU.mult, op1=ALU.mult)
                    nc.vector.drain().then_inc(dt_ready, 1)
                elif step == "cum":
                    dve.wait_ge(cum_done, l + 1)
                    nc.vector.tensor_copy(acum, ps[:, 3, ACC:ACC + TT * SH].rearrange("p (t h) -> p t h", t=TT))
                    nc.vector.drain()
                    nc.vector.tensor_tensor(dsub, ps[:, 3, ALC:ALC + SH], acum[:, 0, :], ALU.subtract)
                    nc.vector.drain().then_inc(cum_sub, 1)
                elif step == "tok":
                    dve.wait_ge(tok_act, l + 1)
                    for t in range(TT):
                        nc.vector.tensor_tensor(heads(xdt[:, t, :]), heads(xs_tok[:, t, :]), per_head(dtr[:, t, :]), ALU.mult)
                    nc.vector.drain()
                    dve.wait_ge(cum_exp, l + 1)
                    nc.vector.tensor_tensor(heads(xdte), heads(xdt[:, 0, :]), per_head(dend), ALU.mult)
                    nc.vector.drain().then_inc(tok_dve, 1)
                elif step == "decay":
                    dve.wait_ge(row_done, 2 * l + i + 1)
                    for h in range(SH):
                        nc.vector.scalar_tensor_tensor(out=decay[:, h, :], in0=pair(4)[:, h * P:(h + 1) * P],
                                                       scalar=acum[:, i, h:h + 1], in1=maskT[:],
                                                       op0=ALU.subtract, op1=ALU.add)
                    nc.vector.drain().then_inc(seg_ready, 1)
                    dve.wait_ge(dec_ready, 2 * l + i + 1)
                    for g in range(SG):
                        cb = ps[:, 3, CBC + g * P:CBC + (g + 1) * P].unsqueeze(1).to_broadcast([P, 4, P])
                        nc.vector.tensor_tensor(decay[:, 4 * g:4 * g + 4, :], decay[:, 4 * g:4 * g + 4, :], cb, ALU.mult)
                    nc.vector.drain().then_inc(mt_ready, 1)
                elif step == "ssd":
                    dskip = per_head(small[:, D_SKIP, SH * l:SH * (l + 1)])
                    nc.vector.tensor_tensor(heads(xs_tok[:, i, :]), heads(xs_tok[:, i, :]), dskip, ALU.mult)
                    dve.wait_ge(y_done, 2 * l + i + 1)
                    nc.vector.drain()
                    nc.vector.tensor_tensor(ytok[:, i, :], ps[:, 4, :], xs_tok[:, i, :], ALU.add)
                    if i == 1:
                        nc.vector.tensor_tensor(heads(xdt[:, 0, :]), heads(ps[:, 5, :]), per_head(eacum), ALU.mult)
                        nc.vector.drain()
                        nc.vector.tensor_tensor(ytok[:, 1, :], ytok[:, 1, :], xdt[:, 0, :], ALU.add)
                    nc.vector.drain().then_inc(y_out, 1)
                elif step == "ssdnorm":
                    dve.wait_ge(proj_out, NOUT * l + OUTS.index(("z", 1)) + 1)
                    nc.vector.tensor_tensor(ytok, ytok, sz, ALU.mult)
                    nc.vector.drain().then_inc(v_ready, 1)
                    r = rq(l, "ssd")
                    dve.wait_ge(rstd_ready, r + 1)
                    rs = rstd[:, r, 0:TT * SG].unsqueeze(2).to_broadcast([P, TT * SG, 256])
                    yv = ytok.rearrange("p t (g n) -> p (t g) n", g=SG)
                    nc.vector.tensor_tensor(yv, yv, rs, ALU.mult)
                    nc.vector.drain().then_inc(vn_ready, 1)
                elif step == "ssdT":
                    dve.wait_ge(ssdT, l + 1)
                    for j in range(4):
                        nc.vector.tensor_scalar(mixT[:, 4 + j, :], pair(4)[:, j * SEQ:(j + 1) * SEQ],
                                                col(2, ROW_SN + 4 * l + j), None, ALU.mult)
                    nc.vector.drain().then_inc(ssd_mix, 1)
                elif step == "soft":
                    t = i % TT
                    n = P * (t + 1)
                    b = i % 2
                    dve.wait_ge(sc_done, NU * l + i + 1)
                    if NU * l + i >= 2:
                        dve.wait_ge(e_ready, NU * l + i - 1)
                    sc = ps[:, 6, :].rearrange("p (m n) -> p m n", m=2)[:, :, 0:n]
                    mk = maskq[:].rearrange("p a n -> p (a n)")[:, SEQ - n:SEQ].unsqueeze(1).to_broadcast([P, 2, n])
                    nc.vector.tensor_tensor(s_sb[:, b, :, 0:n], sc, mk, ALU.add)
                    nc.vector.drain()
                    nc.vector.tensor_reduce(mx[:, b], s_sb[:, b, :, 0:n], AX.X, ALU.max)
                    nc.vector.drain()
                    nc.vector.tensor_scalar(nb[:, b], mx[:, b], -HD ** -0.5, None, ALU.mult)
                    nc.vector.drain().then_inc(sm_ready, 1)
                elif step == "pt":
                    n = P * (i % TT + 1)
                    b = i % 2
                    dve.wait_ge(e_ready, NU * l + i + 1)
                    nc.vector.reciprocal(er[:, b], es[:, b])
                    nc.vector.drain()
                    nc.vector.tensor_tensor(er[:, b, 1:2], er[:, b, 1:2], nlam[:, l:l + 1], ALU.mult)
                    nc.vector.tensor_scalar(e_sb[:, b, 0, 0:n], e_sb[:, b, 0, 0:n], er[:, b, 0:1], None, ALU.mult)
                    if NU * l + i >= 2:
                        dve.wait_ge(pt_done, NU * l + i - 1)
                    nc.vector.drain()
                    nc.vector.scalar_tensor_tensor(out=pd[:, b, 0:n], in0=e_sb[:, b, 1, 0:n], scalar=er[:, b, 1:2],
                                                   in1=e_sb[:, b, 0, 0:n], op0=ALU.mult, op1=ALU.add)
                    nc.vector.drain().then_inc(pd_ready, 1)
                elif step == "attn":
                    r = rq(l, "attn")
                    dve.wait_ge(rstd_ready, r + 1)
                    rs = rstd[:, r, 0:TT * HEADS].unsqueeze(2).to_broadcast([P, TT * HEADS, P])
                    ov = o_tok.rearrange("p t (h n) -> p (t h) n", h=HEADS)
                    nc.vector.tensor_tensor(ov, ov, rs, ALU.mult)
                    nc.vector.drain().then_inc(on_ready, 1)
                    dve.wait_ge(attT, l + 1)
                    for t in range(TT):
                        nc.vector.tensor_scalar(mixT[:, 0:4, t * P:(t + 1) * P],
                                                ps[:, 6 + t, :].rearrange("p (h n) -> p h n", h=HEADS),
                                                subc[:, l:l + 1], None, ALU.mult)
                    nc.vector.drain().then_inc(att_mix, 1)

            for l in range(DEPTH):
                modulation(l)
                pre_norm(2 * l, "pre_mix")
                for step, i in STEPS:
                    mixer_step(l, step, i)
                post_norm(l, 0, "post_mix", [pair(2 * t) for t in range(TT)])
                pre_norm(2 * l + 1, "pre_ffn")
                if l == 0:
                    for q in range(NQ):
                        dve.wait_ge(f_sl, q + 1)
                        if q >= 2:
                            dve.wait_ge(f_dn, q - 1)
                        b = 2 * (q % 2)
                        nc.vector.tensor_tensor(f_act[:, q % 2], f_silu[:, q % 2],
                                                ps[:, b + 1, :].rearrange("p (j n) -> p j n", j=2),
                                                ALU.mult).then_inc(f_ac, 1)
                    post_norm(l, 1, "post_ffn", [pair(4 + 2 * t) for t in range(TT)])

            nc.vector.memset(y_moe, 0.0)
            dve.wait_ge(lg_done, 1)
            nc.vector.tensor_copy(lg, ps[:, 6, 0:TT * NE].rearrange("p (t e) -> p t e", t=TT))
            nc.vector.drain()
            for t in range(TT):
                nc.vector.max(lmx[:, t, :], lg[:, t, :])
            nc.vector.drain()
            for t in range(TT):
                nc.vector.max_index(lix[:, t, :], lmx[:, t, :], lg[:, t, :])
            nc.vector.tensor_tensor(ldel, lmx[:, :, 1], lmx[:, :, 0], ALU.subtract)
            nc.vector.drain()
            nc.vector.tensor_copy(lixf, lix[:, :, 0:2])
            nc.vector.drain()
            for t in range(TT):
                nc.vector.tensor_scalar(oh1[:, t, :], iota[:, 0:NE], lixf[:, t, 0:1], None, ALU.is_equal)
                nc.vector.tensor_scalar(oh2[:, t, :], iota[:, 0:NE], lixf[:, t, 1:2], None, ALU.is_equal)
            nc.vector.drain()
            nc.vector.tensor_tensor(msk, oh1, oh2, ALU.add)
            nc.vector.drain().then_inc(r_del, 1)
            dve.wait_ge(r_exp, 1)
            nc.vector.tensor_scalar(lden, led, 1.0, None, ALU.add)
            nc.vector.drain()
            nc.vector.reciprocal(lg1, lden)
            nc.vector.drain()
            nc.vector.tensor_tensor(lg2, lg1, led, ALU.mult)
            nc.vector.drain()
            for t in range(TT):
                nc.vector.tensor_scalar(oh2[:, t, :], oh2[:, t, :], lg2[:, t:t + 1], None, ALU.mult)
            nc.vector.drain()
            for t in range(TT):
                nc.vector.scalar_tensor_tensor(out=gts[:, t, :], in0=oh1[:, t, :], scalar=lg1[:, t:t + 1],
                                               in1=oh2[:, t, :], op0=ALU.mult, op1=ALU.add)
            dve.wait_ge(pos_done, 1)
            pos = ps[:, 6, 16:16 + TT * NE].rearrange("p (t e) -> p t e", t=TT)
            nc.vector.tensor_copy(posj[:, :, 0:NE], pos)
            nc.vector.tensor_copy(mskj[:, :, 0:NE], msk)
            nc.vector.tensor_copy(cnts, ps[:, 6, 32:32 + NE])
            nc.vector.tensor_copy(ejobf[:, 0:NE], iota[:, 0:NE])
            nc.vector.drain()
            nc.vector.tensor_copy(gtsj[:, :, 0:NE], gts)
            nc.vector.tensor_scalar(over, cnts, float(P), None, ALU.is_gt)
            nc.vector.drain()
            nc.vector.tensor_tensor_scan(ranki, ones[:, 0:NE], over, 0.0, ALU.mult, ALU.add)
            nc.vector.drain()
            nc.vector.tensor_tensor(rank, ranki, over, ALU.subtract)
            nc.vector.tensor_scalar(njf, ranki[:, NE - 1:NE], float(NE), None, ALU.add)
            nc.vector.drain()
            for k in range(EXTRA):
                nc.vector.scalar_tensor_tensor(out=ohk[:, k, :], in0=rank, scalar=float(k), in1=over,
                                               op0=ALU.is_equal, op1=ALU.mult)
            nc.vector.drain()
            nc.vector.tensor_tensor(epick, ohk, iota[:, 0:NE].unsqueeze(1).to_broadcast([P, EXTRA, NE]), ALU.mult)
            nc.vector.drain()
            nc.vector.tensor_reduce(ejobf[:, NE:NJOB], epick, AX.X, ALU.add)
            for src, dst in ((posj, posj), (mskj, mskj), (gtsj, gtsj)):
                for t in range(TT):
                    nc.vector.tensor_tensor(pick[:, t], src[:, t, 0:NE].unsqueeze(1).to_broadcast([P, EXTRA, NE]),
                                            ohk, ALU.mult)
                nc.vector.drain()
                nc.vector.tensor_reduce(dst[:, :, NE:NJOB], pick, AX.X, ALU.add)
                nc.vector.drain()
            nc.vector.tensor_scalar(posj[:, :, NE:NJOB], posj[:, :, NE:NJOB], -float(P), None, ALU.add)
            nc.vector.tensor_copy(ejob[:], ejobf)
            nc.vector.tensor_copy(njob[:], njf)
            nc.vector.drain().then_inc(routed, 1)

            dve.wait_ge(routed, 1)
            n_jobs = dve.value_load(njob[0:1, 0:1], min_val=NE, max_val=NJOB)
            with dve.Fori(0, n_jobs) as job:
                for t in range(TT):
                    one = lambda a: a[:, t, bass.ds(job, 1)]
                    nc.vector.tensor_scalar(sel[:, t, :], iota[:], one(posj), one(mskj), ALU.is_equal, ALU.mult)
                    nc.vector.tensor_scalar(selg[:, t, :], iota[:], one(posj), one(gtsj), ALU.is_equal, ALU.mult)
                nc.vector.drain().then_inc(sel_ready, 1)
                for ch in range(NCH):
                    dve.wait_ge(m_sl, job * NCH + (ch + 1))
                    nc.vector.tensor_tensor(m_act[:, ch % 2, :], m_silu, ps[:, 2 * (ch % 2) + 1, :],
                                            ALU.mult).then_inc(m_ac, 1)
                for g in range(4):
                    t, half = g // 2, g % 2
                    dve.wait_ge(sca_done, job * 4 + (g + 1))
                    y = y_moe[:, t, half * 512:(half + 1) * 512]
                    nc.vector.tensor_tensor(y, y, ps[:, 6 + g % 2, :], ALU.add).then_inc(sca_out, 1)
            nc.vector.drain().then_inc(ysub_done, 1)
            post_norm(DEPTH - 1, 1, "post_ffn", [y_moe[:, t, :] for t in range(TT)])

        @block.tensor
        def _(pe):
            used = [0]

            def weights(tag):
                n = used[0]
                assert stream[n][0] == tag, (stream[n][0], tag)
                pe.wait_ge(landed[n % RING], 16 * (n // RING + 1))
                used[0] += 1
                return ring[:, n % RING, :].rearrange("p (a b) -> p a b", a=stream[n][1].shape[1])

            mm = nc.tensor.matmul
            pe.wait_ge(par_landed, 18 * 16)
            pe.wait_ge(consts, 1)
            pe.wait_ge(zeroed, 1)
            for i in range(3):
                last = nc.tensor.transpose(ps[:, 7, i * P:(i + 1) * P], praw[:, i, :], ident[:])
            last.then_inc(parT, 1)

            def modulation(l):
                pe.wait_ge(c_ready, 1)
                for i in range(NM // 2):
                    w = weights(("mod", l, i))
                    for j in range(2):
                        m = 2 * i + j
                        for k in range(KT):
                            last = mm(ps[:, 3, m:m + 1], w[:, k, j * P:(j + 1) * P], c_act[:, k:k + 1],
                                      start=(k == 0), stop=(k == KT - 1))
                    last.then_inc(w_used, 1)
                nc.tensor.drain().then_inc(mod_done, 1)

            def gate_rows(l):
                pe.wait_ge(mod_ready, l + 1)
                if l:
                    pe.wait_ge(x_ready, 2 * l)
                for s in range(2):
                    b = 6 if s == 0 else 4
                    for j in range(KT):
                        last = mm(pair(b)[:, j * P:(j + 1) * P], gcol[:, l, s, j:j + 1].to_broadcast([P, P]), ident[:],
                                  start=True, stop=True)
                    last.then_inc(grow_done, 1)

            def pre_norm(n):
                pe.wait_ge(xn_ready, n + 1)
                if n % 2 == 0:
                    pe.wait_ge(grow_ready, n + 2)
                for g in range(4):
                    if g >= 2:
                        pe.wait_ge(hT_ready, 4 * n + g - 1)
                    for j in range(2):
                        for t in range(TT):
                            kt = 2 * g + j
                            last = nc.tensor.transpose(ps[:, 4 + g % 2, j * SEQ + t * P:j * SEQ + (t + 1) * P],
                                                       xn[:, t, kt * P:(kt + 1) * P], ident[:])
                    last.then_inc(xnT_ready, 1)
                pe.wait_ge(hT_ready, 4 * n + 4)

            def project(l, i):
                kind, half = OUTS[i]
                n = NOUT * l + i
                if kind in TOKEN_MAJOR:
                    if half:
                        return
                    pe.wait_ge(proj_out, n - 1)
                    for kh in range(2):
                        w = weights((kind, l, kh))
                        for t in range(TT):
                            for k in range(4):
                                kt = 4 * kh + k
                                last = mm(ps[:, (i + t) % 3, :], hT[:, kt, t * P:(t + 1) * P], w[:, k, :],
                                          start=(kt == 0), stop=(kt == KT - 1))
                        last.then_inc(w_used, 1)
                    nc.tensor.drain().then_inc(proj_done, 2)
                    return
                if n >= 3:
                    pe.wait_ge(proj_out, n - 2)
                w = weights((kind, l, half))
                for j in range(2):
                    for k in range(KT):
                        last = mm(ps[:, i % 3, j * SEQ:(j + 1) * SEQ], w[:, k, j * P:(j + 1) * P], hT[:, k, :],
                                  start=(k == 0), stop=(k == KT - 1))
                last.then_inc(w_used, 1)
                nc.tensor.drain().then_inc(proj_done, 1)

            def mixer_step(l, step, i):
                if step == "out":
                    project(l, i)
                elif step == "dt":
                    for t in range(TT):
                        for k in range(KT):
                            last = mm(ps[:, 3, DTC + SH * t:DTC + SH * (t + 1)], hT[:, k, t * P:(t + 1) * P], wdt[:, l, k, :],
                                      start=(k == 0), stop=(k == KT - 1))
                    last.then_inc(dt_mm, 1)
                elif step == "cum":
                    pe.wait_ge(dt_ready, l + 1)
                    for t in range(TT):
                        mm(ps[:, 3, ACC + SH * t:ACC + SH * (t + 1)], upper[:], dA[:, t, :], start=True, stop=True)
                    mm(ps[:, 3, ALC:ALC + SH], ones[:], dA[:, 0, :], start=True, stop=True).then_inc(cum_done, 1)
                elif step == "tok":
                    pe.wait_ge(conv_done, 4 * l + 4)
                    for t in range(TT):
                        for j in range(4):
                            nc.tensor.transpose(ps[:, 4 + t, j * P:(j + 1) * P], convT[:, j, t * P:(t + 1) * P], ident[:])
                    pe.wait_ge(cum_sub, l + 1)
                    for g in range(SG):
                        last = nc.tensor.transpose(ps[:, 3, CBC + g * P:CBC + (g + 1) * P], convT[:, 4 + g, 0:P], ident[:])
                    last.then_inc(tok_done, 1)
                elif step == "decay":
                    if i == 0:
                        pe.wait_ge(tok_dve, l + 1)
                        pe.wait_ge(tok_act, l + 1)
                    else:
                        pe.wait_ge(y_out, 2 * l + 1)
                        pe.wait_ge(st_ready, l + 1)
                    for h in range(SH):
                        mm(pair(4)[:, h * P:(h + 1) * P], dA[:, i, h:h + 1].to_broadcast([P, P]), upper[:],
                           start=True, stop=True)
                    for g in range(SG):
                        last = mm(ps[:, 3, CBC + g * P:CBC + (g + 1) * P], convT[:, 4 + g, i * P:(i + 1) * P],
                                  convT[:, 6 + g, i * P:(i + 1) * P], start=True, stop=True)
                    last.then_inc(row_done, 1)
                elif step == "ssd":
                    pe.wait_ge(mt_ready, 2 * l + i + 1)
                    for h in range(SH):
                        mm(ps[:, 4, h * SP_:(h + 1) * SP_], decay[:, h, :], xdt[:, i, h * SP_:(h + 1) * SP_],
                           start=True, stop=True)
                    for g in range(SG):
                        w = slice(g * 256, (g + 1) * 256)
                        if i == 0:
                            last = mm(ps[:, 5, w], b_tok[:, g, :], xdte[:, w], start=True, stop=True)
                        else:
                            last = mm(ps[:, 5, w], convT[:, 6 + g, P:2 * P], prev[:, w], start=True, stop=True)
                    last.then_inc(y_done, 1)
                elif step == "ssdT":
                    pe.wait_ge(vn_ready, l + 1)
                    for j in range(4):
                        for t in range(TT):
                            last = nc.tensor.transpose(pair(4)[:, j * SEQ + t * P:j * SEQ + (t + 1) * P],
                                                       ytok[:, t, j * P:(j + 1) * P], ident[:])
                    last.then_inc(ssdT, 1)
                elif step == "soft":
                    h, t = i // TT, i % TT
                    n = P * (t + 1)
                    if i == 0:
                        pe.wait_ge(proj_out, NOUT * l + OUTS.index(("v", 1)) + 1)
                        pe.wait_ge(grow_ready, 2 * l + 1)
                    if NU * l + i >= 1:
                        pe.wait_ge(sm_ready, NU * l + i)
                    for m in range(2):
                        o = slice(m * HD, (m + 1) * HD)
                        if m:
                            nc.tensor.drain()
                        last = mm(ps[:, 6, m * SEQ:m * SEQ + n], qT[o, h, t * P:(t + 1) * P], kT[o, h, 0:n],
                                  start=True, stop=True)
                    last.then_inc(sc_done, 1)
                elif step == "pt":
                    pe.wait_ge(pd_ready, NU * l + i + 1)
                    if NU * l + i >= 1:
                        pe.wait_ge(pv_out, NU * l + i)
                    for k in range(i % TT + 1):
                        last = nc.tensor.transpose(ps[:, 7, k * P:(k + 1) * P], pd[:, i % 2, k * P:(k + 1) * P], ident[:])
                    last.then_inc(pt_done, 1)
                elif step == "pv":
                    h, t = i // TT, i % TT
                    pe.wait_ge(pt_ready, NU * l + i + 1)
                    for k in range(t + 1):
                        last = mm(ps[:, 7, 256:384], ptT[:, i % 2, k * P:(k + 1) * P], v_tok[:, k, h * P:(h + 1) * P],
                                  start=(k == 0), stop=(k == t))
                    last.then_inc(pv_done, 1)
                elif step == "attn":
                    pe.wait_ge(on_ready, l + 1)
                    for t in range(TT):
                        for h in range(HEADS):
                            last = nc.tensor.transpose(ps[:, 6 + t, h * P:(h + 1) * P], o_tok[:, t, h * P:(h + 1) * P], ident[:])
                    last.then_inc(attT, 1)

            def out_projection(l):
                pe.wait_ge(proj_out, NOUT * (l + 1))
                for n, r in enumerate(WOUT_ORDER):
                    if r == 4:
                        pe.wait_ge(sc_mix, l + 1)
                    if r == 2:
                        pe.wait_ge(ssd_mix, l + 1)
                    if r == 0:
                        pe.wait_ge(att_mix, l + 1)
                    w = weights(("wout", l, r))
                    for k in range(2):
                        for t in range(TT):
                            for half in range(2):
                                last = mm(ps[:, 2 * t + half, :], mixT[:, 2 * r + k, t * P:(t + 1) * P],
                                          w[:, k, half * 512:(half + 1) * 512], start=(n == 0 and k == 0),
                                          stop=(n == 5 and k == 1))
                    last.then_inc(w_used, 1)
                nc.tensor.drain().then_inc(ysub_done, 1)

            def feed_forward():
                for q in range(NQ + 1):
                    if q < NQ:
                        b = 2 * (q % 2)
                        if q >= 2:
                            pe.wait_ge(f_ac, q - 1)
                        for o, name in enumerate(("f1", "f3")):
                            w = weights((name, q))
                            for j in range(2):
                                for k in range(KT):
                                    last = mm(ps[:, b + o, j * SEQ:(j + 1) * SEQ], w[:, k, j * P:(j + 1) * P], hT[:, k, :],
                                              start=(k == 0), stop=(k == KT - 1))
                            last.then_inc(w_used, 1)
                        nc.tensor.drain().then_inc(f_up, 1)
                    if q:
                        w = weights(("f2", q - 1))
                        pe.wait_ge(f_ac, q)
                        for k in range(2):
                            for t in range(TT):
                                for half in range(2):
                                    last = mm(ps[:, 4 + 2 * t + half, :], f_act[:, (q - 1) % 2, k, t * P:(t + 1) * P],
                                              w[:, k, half * 512:(half + 1) * 512], start=(q == 1 and k == 0),
                                              stop=(q == NQ and k == 1))
                        last.then_inc(w_used, 1)
                        nc.tensor.drain().then_inc(f_dn, 1)
                nc.tensor.drain().then_inc(ysub_done, 1)

            for l in range(DEPTH):
                modulation(l)
                gate_rows(l)
                pre_norm(2 * l)
                for step, i in STEPS:
                    mixer_step(l, step, i)
                out_projection(l)
                pre_norm(2 * l + 1)
                if l == 0:
                    feed_forward()

            for t in range(TT):
                for k in range(KT):
                    last = mm(ps[:, 6, t * NE:(t + 1) * NE], hT[:, k, t * P:(t + 1) * P], wrt[:, k, :],
                              start=(k == 0), stop=(k == KT - 1))
            last.then_inc(lg_done, 1)
            for g in range(4):
                if g >= 2:
                    pe.wait_ge(htok_out, g - 1)
                for k in range(4):
                    last = nc.tensor.transpose(ps[:, 4 + g % 2, k * P:(k + 1) * P],
                                               hT[:, (g % 2) * 4 + k, (g // 2) * P:(g // 2 + 1) * P], ident[:])
                last.then_inc(htok_done, 1)
            pe.wait_ge(r_del, 1)
            mm(ps[:, 6, 16:24], strict[:], msk[:, 0, :], start=True, stop=True)
            mm(ps[:, 6, 24:32], ones[:], msk[:, 0, :], start=True, stop=False)
            mm(ps[:, 6, 24:32], strict[:], msk[:, 1, :], start=False, stop=True)
            mm(ps[:, 6, 32:40], ones[:], msk[:, 0, :], start=True, stop=False)
            mm(ps[:, 6, 32:40], ones[:], msk[:, 1, :], start=False, stop=True).then_inc(pos_done, 1)
            pe.wait_ge(htok_out, 4)
            pe.wait_ge(routed, 1)
            n_jobs = pe.value_load(njob[0:1, 0:1], min_val=NE, max_val=NJOB)
            with pe.Fori(0, n_jobs) as job:
                slot = [0]

                def job_weights(kind):
                    i = slot[0]
                    assert JOB[i][0] == kind
                    n = NS + i
                    pe.wait_ge(landed[n % RING], job * (16 * JOB_SLOTS // RING) + 16 * (n // RING + 1))
                    slot[0] += 1
                    return ring[:, n % RING, :].rearrange("p (a b) -> p a b", a=2 if kind == "w2" else 4)

                pe.wait_ge(sel_ready, job + 1)
                for g in range(2):
                    for k in range(4):
                        kt = 4 * g + k
                        for t in range(TT):
                            last = mm(ps[:, 6 + g, k * P:(k + 1) * P], xn[:, t, kt * P:(kt + 1) * P], sel[:, t, :],
                                      start=(t == 0), stop=(t == TT - 1))
                    last.then_inc(gat_done, 1)
                pe.wait_ge(gat_out, job * 3 + 2)
                for t in range(TT):
                    last = nc.tensor.transpose(ps[:, 7, t * P:(t + 1) * P], selg[:, t, :], ident[:])
                last.then_inc(gat_done, 1)

                for ch in range(NCH + 1):
                    if ch < NCH:
                        b = 2 * (ch % 2)
                        if ch >= 2:
                            pe.wait_ge(m_ac, job * NCH + (ch - 1))
                        for o, kind in enumerate(("w1", "w3")):
                            for kh in range(2):
                                w = job_weights(kind)
                                for k in range(4):
                                    kt = 4 * kh + k
                                    last = mm(ps[:, b + o, :], xeT[:, kt, :], w[:, k, :], start=(kt == 0), stop=(kt == KT - 1))
                                last.then_inc(w_used, 1)
                        nc.tensor.drain().then_inc(m_up, 1)
                    if ch:
                        pe.wait_ge(m_ac, job * NCH + ch)
                        if ch >= 2:
                            pe.wait_ge(m_tc, job * NCH + (ch - 1))
                        for k in range(4):
                            last = nc.tensor.transpose(ps[:, 6, k * P:(k + 1) * P], m_act[:, (ch - 1) % 2, k * P:(k + 1) * P], ident[:])
                        last.then_inc(m_tp, 1)
                        pe.wait_ge(m_tc, job * NCH + ch)
                        for kh in range(2):
                            w = job_weights("w2")
                            for k in range(2):
                                for half in range(2):
                                    last = mm(ps[:, 4 + half, :], m_actT[:, (ch - 1) % 2, 2 * kh + k, :],
                                              w[:, k, half * 512:(half + 1) * 512], start=(ch == 1 and kh + k == 0),
                                              stop=(ch == NCH and kh + k == 2))
                            last.then_inc(w_used, 1)
                nc.tensor.drain().then_inc(m_dn, 1)
                pe.wait_ge(ye_out, job + 1)
                pe.wait_ge(gat_out, job * 3 + 3)
                for g in range(4):
                    t, half = g // 2, g % 2
                    if g >= 2:
                        pe.wait_ge(sca_out, job * 4 + (g - 1))
                    mm(ps[:, 6 + g % 2, :], selgT[:, t, :], y_e[:, half * 512:(half + 1) * 512],
                       start=True, stop=True).then_inc(sca_done, 1)
                pe.wait_ge(sca_out, job * 4 + 4)


_INS = ["x", "c", "w_mod", "b_mod", "norm_mix_pre", "norm_mix_post", "norm_ffn_pre", "norm_ffn_post",
        "w_in", "w_out", "lambda_qk", "attn_subln", "ssd_conv_w", "ssd_conv_b", "ssd_dt_bias",
        "ssd_a_log", "ssd_d", "ssd_norm", "sconv_w", "ffn_w1", "ffn_w3", "ffn_w2",
        "moe_router", "moe_w1", "moe_w3", "moe_w2"]
_OUTS = [((1, SEQ, D), "float32")]


def kernel(**inputs):
    import numpy as _np
    import concourse.bacc as _bacc
    from concourse import mybir as _mybir
    from concourse.bass_utils import run_bass_kernel_spmd as _run

    nc = _bacc.Bacc("TRN2", target_bir_lowering=False, num_devices=1)
    arrays, args = {}, []
    for name in _INS:
        a = _np.ascontiguousarray(inputs[name])
        arrays[f"in_{name}_dram"] = a
        args.append(nc.dram_tensor(f"in_{name}_dram", a.shape, _mybir.dt.from_np(a.dtype), kind="ExternalInput").ap())
    for i, (shape, dtype) in enumerate(_OUTS):
        dt = _mybir.dt.from_np(_np.dtype(dtype))
        args.append(nc.dram_tensor(f"out_{i}_dram", shape, dt, kind="ExternalOutput").ap())
    build(nc, *args)
    r = _run(nc, [arrays], core_ids=[0])
    return r.results[0]["out_0_dram"]
```

```python
import math
from contextlib import ExitStack

import concourse.bass as bass
from concourse import mybir

ALU = mybir.AluOpType
ACT = mybir.ActivationFunctionType
AX = mybir.AxisListType
F32 = mybir.dt.float32
F32R = mybir.dt.float32r
I32 = mybir.dt.int32
U32 = mybir.dt.uint32

P = 128
EPS = 1e-6
NEG = -1e30

D = 1024
SEQ = 256
DEPTH = 2
GW = D // 2
HEADS = 4
HD = GW // (2 * HEADS)
SH, SP_, SG, SN = 8, 64, 2, 128
XBC = GW + 2 * SG * SN
SCONV, CCONV = 3, 4
FF = 2816
NE = 8
FE = 3584
KT = D // P
TT = SEQ // P
NM = 6 * KT

OFF = dict(q=0, k=GW, v=2 * GW, z=3 * GW, xbc=4 * GW, dt=4 * GW + XBC)
OFF["gb"] = OFF["dt"] + SH
OFF["gc"] = OFF["gb"] + GW
OFF["u"] = OFF["gc"] + GW

SLOT = 2048
RING = 6
STAGES = 3
JSTAGES = 6
LEAD = 3
FCH = 512
NCH = FE // FCH
JOB_SLOTS = NCH * 6
EXTRA = 3
NJOB = NE + EXTRA
NQ = FF // 256
NMOD = NM // 2
FIRST_MOD = 2 * KT // 2

OUTS = [("xbc", 0), ("xbc", 1), ("xbc", 2), ("xbc", 3), ("q", 0), ("q", 1), ("k", 0), ("k", 1),
        ("v", 0), ("v", 1), ("gc", 0), ("gc", 1), ("u", 0), ("u", 1), ("gb", 0), ("gb", 1),
        ("z", 0), ("z", 1)]
NOUT = len(OUTS)
TOKEN_MAJOR = ("v", "z")
WOUT_ORDER = [4, 5, 2, 3, 0, 1]
NU = HEADS * TT

AFTER_OUT = {
    0: [("dt", 0), ("conv", 0)], 1: [("conv", 1)], 2: [("conv", 2)], 3: [("conv", 3), ("cum", 0)],
    5: [("tok", 0)], 7: [("decay", 0)],
    9: [("ssd", 0), ("soft", 0), ("pd", 0)],
    10: [("decay", 1), ("pt", 0), ("soft", 1), ("pv", 0), ("pd", 1)],
    11: [("pt", 1), ("soft", 2), ("pv", 1), ("pd", 2)],
    12: [("ssd", 1), ("pt", 2), ("soft", 3), ("pv", 2), ("pd", 3)],
    13: [("pt", 3), ("soft", 4), ("pv", 3), ("pd", 4)],
    14: [("pt", 4), ("soft", 5), ("pv", 4), ("pd", 5)],
    15: [("pt", 5), ("soft", 6), ("pv", 5), ("pd", 6)],
    16: [("sconv", 0), ("pt", 6), ("soft", 7), ("pv", 6), ("pd", 7)],
    17: [("pt", 7), ("ssdnorm", 0), ("pv", 7), ("sconv_split", 0)],
}


def by_pool(l, i):
    return i % 2 == 1 and (l == 1 or i >= FIRST_MOD)


def schedule():
    s = []
    staged = [DEPTH * (NOUT + len(WOUT_ORDER)) + 3 * NQ]

    def split(l=0):
        if staged[0]:
            staged[0] -= 1
            s.append(("split", l, 0))

    def mods(l, a, b):
        for i in range(a, b):
            s.append(("mod", l, i))
            s.append(("modcol", l, i))

    waiting = []

    def finish_mod(pool_too=True):
        for one in list(waiting):
            if pool_too or not by_pool(*one):
                waiting.remove(one)
                s.append(("modcol",) + one)

    def mod(l, i):
        finish_mod(by_pool(l, i))
        s.append(("pmod" if by_pool(l, i) else "mod", l, i))
        waiting.append((l, i))

    mods(0, 0, FIRST_MOD // 2)
    s.append(("xn", 0, 0))
    mods(0, FIRST_MOD // 2, FIRST_MOD)
    s.append(("params", 0, 0))
    s.append(("modfin", 0, 0))
    for _ in range(LEAD):
        split()
    for l in range(DEPTH):
        if l:
            s.append(("xn", l, 0))
        s.append(("norm", l, 0))
        for i in range(NOUT):
            s.append(("out", l, i))
            split(l)
            if l == 0:
                if FIRST_MOD + i < NMOD:
                    mod(l, FIRST_MOD + i)
                elif FIRST_MOD + i == NMOD:
                    finish_mod()
            elif i in (0, 3):
                mod(1, 2 * NQ + i // 3)
            elif i == 6:
                finish_mod()
            s.extend((name, l, j) for name, j in AFTER_OUT.get(i, []))
        s.append(("modfin", l, 1))
        for n in range(len(WOUT_ORDER)):
            if n == 1:
                s.append(("ssdT", l, 0))
            if n == 3:
                s.append(("attn", l, 0))
            if n == 4:
                s.append(("grow", l, 0))
            s.append(("wout", l, n))
            split(l)
        s.append(("post", l, 0))
        s.append(("xn", l, 1))
        s.append(("norm", l, 1))
        s.append(("grow", l, 1))
        if l == 0:
            for q in range(NQ + 1):
                if q < NQ:
                    s.append(("up", l, q))
                    split(l)
                    mod(1, 2 * q)
                    s.append(("gate", l, q))
                    split(l)
                if q:
                    s.append(("down", l, q - 1))
                    split(l)
                if q < NQ:
                    mod(1, 2 * q + 1)
            finish_mod()
            s.append(("modfin", 1, 0))
            s.append(("post", l, 1))
    return s


RMS = ["pre_mix", "ssd", "attn", "post_mix", "pre_ffn", "post_ffn"]
RMS_OF = dict(pre_mix=D, ssd=GW // SG, attn=2 * HD, post_mix=D, pre_ffn=D, post_ffn=D)


def lam_init(layer):
    return 0.8 - 0.6 * math.exp(-0.3 * layer)


def build(nc, x, c, w_mod, b_mod, norm_mix_pre, norm_mix_post, norm_ffn_pre, norm_ffn_post,
          w_in, w_out, lambda_qk, attn_subln, ssd_conv_w, ssd_conv_b, ssd_dt_bias,
          ssd_a_log, ssd_d, ssd_norm, sconv_w, ffn_w1, ffn_w3, ffn_w2,
          moe_router, moe_w1, moe_w3, moe_w2, out):

    def k_rows(w, k0, nk, col, n):
        return w.rearrange("(t p) n -> p t n", p=P)[:, k0:k0 + nk, col:col + n]

    def out_slot(l, i):
        kind, half = OUTS[i]
        if kind in TOKEN_MAJOR:
            return k_rows(w_in[l], half * 4, 4, OFF[kind], 512)
        return k_rows(w_in[l], 0, KT, OFF[kind] + 256 * half, 256)

    SCHED = schedule()
    of_step = {"out": out_slot,
               "wout": lambda l, n: k_rows(w_out[l], 2 * WOUT_ORDER[n], 2, 0, D),
               "up": lambda l, q: k_rows(ffn_w1[0], 0, KT, q * 256, 256),
               "gate": lambda l, q: k_rows(ffn_w3[0], 0, KT, q * 256, 256),
               "down": lambda l, q: k_rows(ffn_w2[0], 2 * q, 2, 0, D)}
    staged_src = [of_step[name](l, i) for name, l, i in SCHED if name in of_step]
    ND = len(staged_src)
    stream = []
    n_mod = n_st = 0
    for name, l, i in SCHED:
        if name == "mod":
            stream.append((True, n_mod, k_rows(w_mod[l], 0, KT, i * 256, 256)))
            n_mod += 1
        elif name == "split":
            stream.append((False, n_st, staged_src[n_st]))
            n_st += 1
    NS = len(stream)
    stream_of = [n for n, (is_mod, _, _) in enumerate(stream) if not is_mod]
    stream_of_mod = [n for n, (is_mod, _, _) in enumerate(stream) if is_mod]
    assert n_st == ND and not any(m for m, _, _ in stream[-RING:])

    JOB = []
    for _ch in range(NCH + 1):
        if _ch < NCH:
            JOB += [("w1", _ch, 0), ("w1", _ch, 1), ("w3", _ch, 0), ("w3", _ch, 1)]
        if _ch:
            JOB += [("w2", _ch - 1, 0), ("w2", _ch - 1, 1)]
    assert len(JOB) == JOB_SLOTS and JOB_SLOTS % RING == 0 and JOB_SLOTS % JSTAGES == 0
    w1_v = moe_w1[0].rearrange("e (t p) n -> e p t n", p=P)
    w3_v = moe_w3[0].rearrange("e (t p) n -> e p t n", p=P)
    w2_v = moe_w2[0].rearrange("e (t p) n -> e p t n", p=P)

    def job_source(e, kind, ch, half):
        if kind == "w2":
            return w2_v[bass.ds(e, 1), :, ch * 4 + half * 2:ch * 4 + half * 2 + 2, :].rearrange("e p t n -> (e p) t n")
        v = w1_v if kind == "w1" else w3_v
        return v[bass.ds(e, 1), :, half * 4:half * 4 + 4, ch * FCH:(ch + 1) * FCH].rearrange("e p t n -> (e p) t n")

    with ExitStack() as ctx:
        def sb(name, shape, dt=F32, stack=ctx):
            return stack.enter_context(nc.sbuf_tensor(name, shape, dt))

        def sem(name):
            return ctx.enter_context(nc.semaphore(name))

        with ExitStack() as loading:
            ring = sb("weight_ring", [P, RING, SLOT], F32, loading)
        ring_lo = sb("lo_ring", [P, RING, SLOT], F32R)
        st_hi = [sb(f"stage_hi{i}", [P, SLOT], F32R) for i in range(STAGES)]
        x_tok = sb("x_tok", [P, TT, D])
        xn = sb("xn", [P, TT, D])
        h_hi = sb("h_hi", [P, KT, SEQ], F32R)
        h_lo = sb("h_lo", [P, KT, SEQ], F32R)
        qk = sb("qk", [P, KT, SEQ])
        praw = sb("praw", [P, 3, P])
        pcol = sb("pcol", [P, 3 * P])
        gate_row = sb("gate_row", [P, D])
        modc = sb("modc", [P, DEPTH, NM])
        acol = sb("acol", [P, DEPTH, 2, KT])
        gcol = sb("gcol", [P, DEPTH, 2, KT])
        subc = sb("subc", [P, DEPTH])
        pm = sb("pool_mod", [P, 2, KT // 2, 256])
        macc = sb("macc", [P, 2, 256])
        c_raw = sb("c_raw", [P, KT])
        c_act = sb("c_act", [P, KT])
        ident = sb("ident", [P, P])
        ones = sb("ones", [P, P])
        upper = sb("upper", [P, P])
        strict = sb("strict", [P, P])
        maskT = sb("maskT", [P, P])
        maskq = sb("maskq", [P, 2, P])
        iota = sb("iota", [P, P])
        neghalf = sb("neghalf", [P, 8])
        small = sb("small", [P, 3, DEPTH * SH])
        lamq = sb("lamq", [P, DEPTH, 4, HD])
        lamp = sb("lamp", [P, DEPTH, 2, HD])
        lams = sb("lams", [P, DEPTH, 2])
        lame = sb("lame", [P, DEPTH, 2])
        nlam = sb("nlam", [P, DEPTH])
        aexp = sb("aexp", [P, DEPTH * SH])
        wdt = sb("wdt", [P, DEPTH, KT, SH])
        wrt = sb("wrt", [P, KT, NE])
        sumsq = sb("sumsq", [P, DEPTH * len(RMS), 8])
        msq = sb("msq", [P, DEPTH * len(RMS), 8])
        rstd = sb("rstd", [P, DEPTH * len(RMS), 8])
        lix = sb("lix", [P, TT, NE], U32)
        ejob = sb("ejob", [P, NJOB], I32)
        njob = sb("njob", [P, 1], I32)
        hT = qk
        qT, kT = qk[:, 0:HEADS, :], qk[:, HEADS:, :]
        ytok, o_tok = xn[:, :, 0:GW], xn[:, :, GW:]

        PADX = CCONV - 1
        PADU = SCONV - 1
        mixer = ExitStack()
        m = lambda name, shape, dt=F32: sb(name, shape, dt, mixer)
        xbcT = m("xbcT", [P, 8, PADX + SEQ])
        convT = xbcT[:, :, PADX:]
        cacc = m("cacc", [P, 2, SEQ])
        v_tok = m("v_tok", [P, TT, GW])
        sz = m("sz", [P, TT, GW])
        gcT = m("gcT", [P, 4, SEQ])
        uT = m("uT", [P, 4, PADU + SEQ])
        gbT = m("gbT", [P, 4, SEQ])
        sc_hi = m("sc_hi", [P, 4, SEQ], F32R)
        sc_lo = m("sc_lo", [P, 4, SEQ], F32R)
        xs_tok = m("xs_tok", [P, TT, GW])
        xdt = m("xdt", [P, TT, GW])
        xdte = m("xdte", [P, GW])
        b_tok = m("b_tok", [P, SG, SN])
        decay = m("decay", [P, SH, P])
        prev = m("prev", [P, GW])
        s_sb = m("s_sb", [P, 2, 2, SEQ])
        e_sb = m("e_sb", [P, 2, 2, SEQ])
        pd = m("pd", [P, 2, SEQ])
        ptT = m("ptT", [P, 2, SEQ])
        dtr, dta, dte_, dtu, dtl, dtz, dtv, dA, acum = (m(n, [P, TT, SH]) for n in (
            "dtr", "dta", "dte", "dtu", "dtl", "dtz", "dtv", "dA", "acum"))
        dsub, dend, eacum = (m(n, [P, SH]) for n in ("dsub", "dend", "eacum"))
        pacc = praw[:, 0:2, :].rearrange("p a b -> p (a b)")
        s_tap = praw[:, 0:2, :].rearrange("p a b -> p (a b)")
        mx, nb, es, er = (m(n, [P, 2, 2]) for n in ("mx", "nb", "es", "er"))
        ssd_mixf = xs_tok[:].rearrange("p t (j n) -> p (t j) n", n=SEQ)
        att_mixf = sz[:].rearrange("p t (j n) -> p (t j) n", n=SEQ)
        mixer.close()

        dense = ExitStack()
        m = lambda name, shape, dt=F32: sb(name, shape, dt, dense)
        f_silu = m("f_silu", [P, 2, SEQ])
        f_act = m("f_act", [P, 2, SEQ])
        f_hi = m("f_hi", [P, 2, 2, SEQ], F32R)
        f_lo = m("f_lo", [P, 2, 2, SEQ], F32R)
        dense.close()

        m = sb
        jst_hi = st_hi + [m(f"stage_hi{i}", [P, SLOT], F32R) for i in range(STAGES, JSTAGES)]
        y_moe = m("y_moe", [P, TT, D])
        xe_hi = m("xe_hi", [P, KT, P], F32R)
        xe_lo = m("xe_lo", [P, KT, P], F32R)
        m_silu = m("m_silu", [P, FCH])
        m_act = m("m_act", [P, 2, FCH])
        a_hi = m("a_hi", [P, 4, P], F32R)
        a_lo = m("a_lo", [P, 4, P], F32R)
        y_e = m("y_e", [P, D])
        sel = m("sel", [P, TT, P], F32R)
        selg = m("selg", [P, TT, P])
        selgT = m("selgT", [P, TT, P])
        lg, lmx, oh1, oh2, msk, gts = (m(n, [P, TT, NE]) for n in ("lg", "lmx", "oh1", "oh2", "msk", "gts"))
        lixf = m("lixf", [P, TT, 2])
        ldel, led, lden, lg1, lg2 = (m(n, [P, TT]) for n in ("ldel", "led", "lden", "lg1", "lg2"))
        posj, mskj, gtsj = (m(n, [P, TT, NJOB + 1]) for n in ("posj", "mskj", "gtsj"))
        cnts, over, ranki, rank = (m(n, [P, NE]) for n in ("cnts", "over", "ranki", "rank"))
        ohk = m("ohk", [P, EXTRA, NE])
        pick = m("pick", [P, TT, EXTRA, NE])
        epick = m("epick", [P, EXTRA, NE])
        ejobf = m("ejobf", [P, NJOB])
        njf = m("njf", [P, 1])
        ht_hi = h_hi[:].rearrange("p k s -> p (k s)").rearrange("p (t d) -> p t d", t=TT)
        ht_lo = h_lo[:].rearrange("p k s -> p (k s)").rearrange("p (t d) -> p t d", t=TT)

        ps = ctx.enter_context(nc.psum_tensor("ps", [P, 8, 512], F32))

        def pair(b):
            return ps[:, b:b + 2, :].rearrange("p b n -> p (b n)")

        def mods_until(l, i):
            pool_ones = sum(by_pool(ll, ii) for ll in range(l + 1) for ii in range(i if ll == l else NMOD))
            return NMOD * l + i - pool_ones, pool_ones

        def mod_bank(l, i):
            return 3 if l and i < FIRST_MOD else 2

        SSDB = 3
        DTC, ACC, ALC, CBC = 0, 16, 32, 256
        UPB, GATEB, TPB, YB = 0, 1, 2, 4
        FREE = [3, 6, 7, 3]

        landed = [sem(f"weights_landed{i}") for i in range(RING)]
        hi_ready = sem("hi_ready")
        lo_ready = sem("lo_ready")
        st_used = sem("st_used")
        pm_landed = [sem(f"pool_mod_landed{i}") for i in range(2)]
        c_landed = sem("c_landed")
        pcol_done = sem("pcol_done")
        pacc_ready = sem("pacc_ready")
        macc_ready = sem("macc_ready")
        mcol_done = sem("mcol_done")
        x_landed = sem("x_landed")
        par_landed = sem("par_landed")
        consts = sem("consts")
        zeroed = sem("zeroed")
        parT = sem("parT")
        pars = sem("pars")
        c_ready = sem("c_ready")
        lam_s = sem("lam_s")
        lam_e = sem("lam_e")
        mod_ready = sem("mod_ready")
        grow_done = sem("grow_done")
        grow_ready = sem("grow_ready")
        ss_ready = sem("ss_ready")
        rstd_ready = sem("rstd_ready")
        xn_ready = sem("xn_ready")
        xnT_ready = sem("xnT_ready")
        hT_ready = sem("hT_ready")
        hh_ready = sem("hh_ready")
        hl_ready = sem("hl_ready")
        proj_done = sem("proj_done")
        proj_out = sem("proj_out")
        conv_acc = sem("conv_acc")
        conv_done = sem("conv_done")
        dt_mm = sem("dt_mm")
        dt_a = sem("dt_a")
        dt_e = sem("dt_e")
        dt_ready = sem("dt_ready")
        cum_done = sem("cum_done")
        cum_sub = sem("cum_sub")
        cum_exp = sem("cum_exp")
        tok_done = sem("tok_done")
        tok_act = sem("tok_act")
        xdt_ready = sem("xdt_ready")
        row_done = sem("row_done")
        seg_ready = sem("seg_ready")
        dec_ready = sem("dec_ready")
        mt_ready = sem("mt_ready")
        y_done = sem("y_done")
        y_out = sem("y_out")
        state_ready = sem("state_ready")
        v_ready = sem("v_ready")
        vn_ready = sem("vn_ready")
        ssdT = sem("ssdT")
        sconv_ready = sem("sconv_ready")
        mixf_ready = sem("mixf_ready")
        mixh_ready = sem("mixh_ready")
        mixl_ready = sem("mixl_ready")
        sc_done = sem("sc_done")
        sm_ready = sem("sm_ready")
        e_ready = sem("e_ready")
        pd_ready = sem("pd_ready")
        pt_done = sem("pt_done")
        pt_ready = sem("pt_ready")
        pv_done = sem("pv_done")
        pv_out = sem("pv_out")
        on_ready = sem("on_ready")
        attT = sem("attT")
        ysub_done = sem("ysub_done")
        x_ready = sem("x_ready")
        f_up = sem("f_up")
        f_gt = sem("f_gt")
        f_sl = sem("f_sl")
        f_ac = sem("f_ac")
        f_h = sem("f_h")
        f_l = sem("f_l")
        f_dn = sem("f_dn")
        htok_done = sem("htok_done")
        htok_h = sem("htok_h")
        htok_l = sem("htok_l")
        lg_done = sem("lg_done")
        r_del = sem("r_del")
        r_exp = sem("r_exp")
        pos_done = sem("pos_done")
        routed = sem("routed")
        sel_ready = sem("sel_ready")
        gat_done = sem("gat_done")
        xh_ready = sem("xh_ready")
        xl_ready = sem("xl_ready")
        sgt_done = sem("sgt_done")
        sgt_ready = sem("sgt_ready")
        m_up = sem("m_up")
        m_gt = sem("m_gt")
        m_sl = sem("m_sl")
        m_ac = sem("m_ac")
        m_tp = sem("m_tp")
        m_th = sem("m_th")
        m_tl = sem("m_tl")
        m_dn = sem("m_dn")
        ye_out = sem("ye_out")
        sca_done = sem("sca_done")
        sca_out = sem("sca_out")
        stored = sem("stored")

        block = ctx.enter_context(nc.Block())

        def rq(l, name):
            return l * len(RMS) + RMS.index(name)

        def col(tile, row):
            return pcol[:, tile * P + row:tile * P + row + 1]

        def cols(tile, row, n):
            return pcol[:, tile * P + row:tile * P + row + n]

        ROW_BMOD = 8
        GAIN = {"pre_mix": 0, "post_mix": 16, "pre_ffn": 32, "post_ffn": 48}
        ROW_CW = 64
        ROW_CB, ROW_SW, ROW_SN, ROW_AS = 0, 16, 40, 48
        DT_BIAS, A_LOG, D_SKIP = range(3)
        NOUT_Z = OUTS.index(("z", 1)) + 1
        NOUT_V = OUTS.index(("v", 1)) + 1
        NOUT_GB = OUTS.index(("gb", 1)) + 1

        @block.sync
        def _(sp):
            sp.dma_start(c_raw[:], c.rearrange("b (t p) -> p (b t)", p=P), allow_slow_non_contiguous=True).then_inc(c_landed, 16)
            for n, (_, _, src) in enumerate(stream):
                if n == 2:
                    sp.dma_start(x_tok[:], x.rearrange("b (t p) d -> p (b t) d", p=P)).then_inc(x_landed, 16)
                if n >= RING:
                    was_mod, i, _ = stream[n - RING]
                    sp.wait_ge(macc_ready if was_mod else st_used, i + 1)
                sp.dma_start(ring[:, n % RING, :].rearrange("p (a b) -> p a b", a=src.shape[1]),
                             src).then_inc(landed[n % RING], 16)

            def load_expert(job, e):
                for i, (kind, ch, half) in enumerate(JOB):
                    s = (NS + i) % RING
                    sp.wait_ge(st_used, job * JOB_SLOTS + (ND + i - RING + 1))
                    src = job_source(e, kind, ch, half)
                    sp.dma_start(ring[:, s, :].rearrange("p (a b) -> p a b", a=src.shape[1]),
                                 src).then_inc(landed[s], 16)

            with sp.Fori(0, NE) as e:
                load_expert(e, e)
            sp.wait_ge(routed, 1)
            n_jobs = sp.value_load(njob[0:1, 0:1], min_val=NE, max_val=NJOB)
            with sp.If(n_jobs > NE):
                with sp.Fori(NE, n_jobs) as job:
                    e = sp.value_load(ejob[0:1, bass.ds(job, 1)], min_val=0, max_val=NE - 1)
                    load_expert(job, e)
            sp.wait_ge(x_ready, 2 * DEPTH)
            sp.dma_start(out.rearrange("b (t p) d -> p (b t) d", p=P), x_tok[:]).then_inc(stored, 16)
            sp.wait_ge(stored, 16)

        @block.gpsimd
        def _(pool):
            nc.gpsimd.memset(ones[:], 1.0)
            nc.gpsimd.memset(neghalf[:], -0.5)
            nc.gpsimd.memset(maskq[:], 0.0)
            nc.gpsimd.memset(maskT[:], 0.0)
            nc.gpsimd.memset(ident[:], 0.0)
            nc.gpsimd.drain()
            nc.gpsimd.affine_select(out=ident[:], in_=ident[:], compare_op=ALU.not_equal, fill=1.0,
                                    base=0, pattern=[[-1, P]], channel_multiplier=1)
            nc.gpsimd.affine_select(out=upper[:], in_=ones[:], compare_op=ALU.is_ge, fill=0.0,
                                    base=0, pattern=[[1, P]], channel_multiplier=-1)
            nc.gpsimd.affine_select(out=strict[:], in_=ones[:], compare_op=ALU.is_gt, fill=0.0,
                                    base=0, pattern=[[1, P]], channel_multiplier=-1)
            nc.gpsimd.affine_select(out=maskT[:], in_=maskT[:], compare_op=ALU.is_ge, fill=NEG,
                                    base=0, pattern=[[1, P]], channel_multiplier=-1)
            nc.gpsimd.affine_select(out=maskq[:, 1, :], in_=maskq[:, 1, :], compare_op=ALU.is_ge, fill=NEG,
                                    base=0, pattern=[[-1, P]], channel_multiplier=1)
            nc.gpsimd.iota(iota[:], pattern=[[1, P]], base=0, channel_multiplier=0,
                           allow_small_or_imprecise_dtypes=True)
            nc.gpsimd.drain().then_inc(consts, 1)

            def serve_rms(l, name, n):
                r = rq(l, name)
                pool.wait_ge(ss_ready, r + 1)
                nc.gpsimd.tensor_scalar(msq[:, r, 0:n], sumsq[:, r, 0:n], 1.0 / RMS_OF[name], EPS, ALU.mult, ALU.add)
                nc.gpsimd.drain()
                nc.gpsimd.tensor_tensor(rstd[:, r, 0:n], msq[:, r, 0:n], neghalf[:, 0:n],
                                        ALU.pow).then_inc(rstd_ready, 1)

            sconv_at = [n for n, (name, _, _) in enumerate(SCHED) if name == "sconv"]
            sconv_pmods = [sum(name == "pmod" for name, _, _ in SCHED[:n]) for n in sconv_at]
            halves = [(l, i, half) for name, l, i in SCHED if name == "pmod" for half in range(2)]

            def load_half(n):
                if n < len(halves):
                    l, i, half = halves[n]
                    pool.dma_start(pm[:, n % 2], k_rows(w_mod[l], half * KT // 2, KT // 2, i * 256, 256)
                                   ).then_inc(pm_landed[n % 2], 16)

            load_half(0)
            load_half(1)
            pool.wait_ge(c_ready, 1)
            n_half = 0
            for name, l, i in SCHED:
                if name == "pmod":
                    if n_half == 0:
                        pool.wait_ge(parT, 1)
                    for half in range(2):
                        n = n_half
                        w = pm[:, n % 2]
                        pool.wait_ge(pm_landed[n % 2], 16 * (n // 2 + 1))
                        cb = c_act[:, half * 4:half * 4 + 4].unsqueeze(2).to_broadcast([P, KT // 2, 256])
                        nc.gpsimd.tensor_tensor(w, w, cb, ALU.mult)
                        nc.gpsimd.drain()
                        nc.gpsimd.tensor_tensor(w[:, 0:2, :], w[:, 0:2, :], w[:, 2:4, :], ALU.add)
                        nc.gpsimd.drain()
                        if half:
                            nc.gpsimd.tensor_tensor(w[:, 0, :], w[:, 0, :], w[:, 1, :], ALU.add)
                            nc.gpsimd.drain()
                            nc.gpsimd.tensor_tensor(pacc, pacc, w[:, 0, :], ALU.add)
                            nc.gpsimd.drain().then_inc(pacc_ready, 1)
                        else:
                            if n:
                                pool.wait_ge(pcol_done, n // 2)
                            nc.gpsimd.tensor_tensor(pacc, w[:, 0, :], w[:, 1, :], ALU.add)
                            nc.gpsimd.drain()
                        load_half(n + 2)
                        n_half += 1
                elif name == "xn":
                    serve_rms(l, ("pre_mix", "pre_ffn")[i], TT)
                elif name == "ssdnorm":
                    serve_rms(l, "ssd", TT * SG)
                elif name == "attn":
                    serve_rms(l, "attn", TT * HEADS)
                elif name == "post":
                    serve_rms(l, ("post_mix", "post_ffn")[i], TT)
                elif name == "sconv":
                    pool.wait_ge(proj_out, NOUT * l + NOUT_GB)
                    nc.gpsimd.memset(uT[:, :, 0:PADU], 0.0)
                    nc.gpsimd.tensor_tensor(uT[:, :, PADU:], uT[:, :, PADU:], gcT[:], ALU.mult)
                    nc.gpsimd.drain()
                    pool.wait_ge(pcol_done, sconv_pmods[l])
                    for j in range(4):
                        nc.gpsimd.tensor_scalar(gcT[:, j, :], uT[:, j, 0:SEQ],
                                                col(2, ROW_SW + 12 * l + j), None, ALU.mult)
                    for k in range(1, SCONV):
                        for j in range(4):
                            nc.gpsimd.tensor_scalar(s_tap, uT[:, j, k:k + SEQ],
                                                    col(2, ROW_SW + 12 * l + 4 * k + j), None, ALU.mult)
                            nc.gpsimd.drain()
                            nc.gpsimd.tensor_tensor(gcT[:, j, :], gcT[:, j, :], s_tap, ALU.add)
                            nc.gpsimd.drain()
                    nc.gpsimd.tensor_tensor(gbT[:], gcT[:], gbT[:], ALU.mult)
                    nc.gpsimd.drain().then_inc(sconv_ready, 1)
            serve_rms(DEPTH - 1, "post_ffn", TT)

        @block.scalar
        def _(act):
            act.wait_ge(zeroed, 1)
            loads = [(0, ROW_BMOD, b_mod.rearrange("l (t p) -> (l t) p", p=P)),
                     (1, GAIN["pre_mix"], norm_mix_pre.rearrange("l (t p) -> (l t) p", p=P)),
                     (1, GAIN["post_mix"], norm_mix_post.rearrange("l (t p) -> (l t) p", p=P)),
                     (1, GAIN["pre_ffn"], norm_ffn_pre.rearrange("l (t p) -> (l t) p", p=P)),
                     (1, GAIN["post_ffn"], norm_ffn_post.rearrange("l (t p) -> (l t) p", p=P)),
                     (1, ROW_CW, ssd_conv_w.rearrange("l k (t p) -> (l k t) p", p=P)),
                     (2, ROW_CB, ssd_conv_b.rearrange("l (t p) -> (l t) p", p=P)),
                     (2, ROW_SW, sconv_w.rearrange("l k (t p) -> (l k t) p", p=P)),
                     (2, ROW_SN, ssd_norm.rearrange("l (t p) -> (l t) p", p=P)),
                     (2, ROW_AS, attn_subln)]
            for tile, row, src in loads:
                act.dma_start(praw[row:row + src.shape[0], tile, :], src).then_inc(par_landed, 16)
            for i, v in enumerate((ssd_dt_bias, ssd_a_log, ssd_d)):
                act.dma_start(small[:, i, :], v.rearrange("l h -> (l h)").partition_broadcast(P)).then_inc(par_landed, 16)
            act.dma_start(lamq[:].rearrange("p l f d -> p (l f d)"),
                          lambda_qk.rearrange("l f d -> (l f d)").partition_broadcast(P)).then_inc(par_landed, 16)
            for l in range(DEPTH):
                act.dma_start(wdt[:, l], k_rows(w_in[l], 0, KT, OFF["dt"], SH)).then_inc(par_landed, 16)
            act.dma_start(wrt[:], k_rows(moe_router[0], 0, KT, 0, NE)).then_inc(par_landed, 16)

            act.wait_ge(c_landed, 16)
            nc.scalar.activation(c_act[:], c_raw[:], ACT.Silu).then_inc(c_ready, 1)

            def squares(l, name, parts, scratch):
                r = rq(l, name)
                for i, a in enumerate(parts):
                    if i and i % len(scratch) == 0:
                        nc.scalar.drain()
                    nc.scalar.activation(scratch[i % len(scratch)], a, ACT.Square, accum_out=sumsq[:, r, i:i + 1])
                nc.scalar.drain().then_inc(ss_ready, 1)

            xn_scratch = [xn[:, t, :] for t in range(TT)]

            def copy_projection(l, i):
                kind, half = OUTS[i]
                if kind in TOKEN_MAJOR and not half:
                    return
                act.wait_ge(proj_done, NOUT * l + i + 1)
                if kind == "v":
                    nc.scalar.copy(v_tok[:], ps[:, 0:TT, :]).then_inc(proj_out, 2)
                    return
                if kind == "z":
                    nc.scalar.activation(sz[:], ps[:, 0:TT, :], ACT.Silu).then_inc(proj_out, 2)
                    return
                two = slice(2 * half, 2 * half + 2)
                dst = {"xbc": convT, "q": qT, "k": kT, "gc": gcT, "gb": gbT, "u": uT[:, :, PADU:]}[kind][:, two, :]
                nc.scalar.copy(dst, ps[:, i % 2, :].rearrange("p (j n) -> p j n", j=2)).then_inc(proj_out, 1)

            n_split = 0
            n_mix = 0
            for name, l, i in SCHED:
                if name == "split":
                    n, k = stream_of[n_split], n_split
                    act.wait_ge(landed[n % RING], 16 * (n // RING + 1))
                    if k >= STAGES:
                        act.wait_ge(st_used, k - STAGES + 1)
                    nc.scalar.copy(st_hi[k % STAGES][:], ring[:, n % RING, :]).then_inc(hi_ready, 1)
                    n_split += 1
                elif name == "params":
                    act.wait_ge(pars, 1)
                    nc.scalar.activation(aexp[:], small[:, A_LOG, :], ACT.Exp)
                    act.wait_ge(lam_s, 1)
                    nc.scalar.activation(lame[:], lams[:], ACT.Exp).then_inc(lam_e, 1)
                elif name == "xn":
                    if l or i:
                        act.wait_ge(x_ready, 2 * l + i)
                    else:
                        act.wait_ge(x_landed, 16)
                    squares(l, ("pre_mix", "pre_ffn")[i], [x_tok[:, t, :] for t in range(TT)], xn_scratch)
                elif name == "norm":
                    for g in range(4):
                        act.wait_ge(hT_ready, 4 * (2 * l + i) + g + 1)
                        nc.scalar.copy(h_hi[:, 2 * g:2 * g + 2, :], hT[:, 2 * g:2 * g + 2, :]).then_inc(hh_ready, 1)
                elif name == "out":
                    copy_projection(l, i)
                elif name == "conv":
                    act.wait_ge(conv_acc, 4 * l + i + 1)
                    nc.scalar.activation(convT[:, 2 * i:2 * i + 2, :], cacc[:], ACT.Silu).then_inc(conv_done, 1)
                elif name == "dt":
                    act.wait_ge(dt_a, 2 * l + 1)
                    nc.scalar.activation(dte_[:], dta[:], ACT.Exp).then_inc(dt_e, 1)
                    act.wait_ge(dt_a, 2 * l + 2)
                    nc.scalar.activation(dtl[:], dtu[:], ACT.Ln).then_inc(dt_e, 1)
                elif name == "cum":
                    act.wait_ge(cum_sub, l + 1)
                    nc.scalar.activation(dend[:], dsub[:], ACT.Exp)
                    nc.scalar.activation(eacum[:], acum[:, 1, :], ACT.Exp)
                    nc.scalar.drain().then_inc(cum_exp, 1)
                elif name == "tok":
                    act.wait_ge(tok_done, l + 1)
                    nc.scalar.copy(xs_tok[:], ps[:, 4:6, :])
                    nc.scalar.copy(b_tok[:].rearrange("p g n -> p (g n)"), ps[:, SSDB, CBC:CBC + SG * SN])
                    nc.scalar.drain().then_inc(tok_act, 1)
                elif name == "decay":
                    act.wait_ge(seg_ready, 2 * l + i + 1)
                    nc.scalar.activation(decay[:], decay[:], ACT.Exp).then_inc(dec_ready, 1)
                elif name == "ssd":
                    if i == 0:
                        act.wait_ge(y_done, 2 * l + 1)
                        nc.scalar.copy(prev[:], ps[:, 5, :]).then_inc(state_ready, 1)
                elif name == "ssdnorm":
                    act.wait_ge(v_ready, l + 1)
                    squares(l, "ssd", [ytok[:, t, g * 256:(g + 1) * 256] for t in range(TT) for g in range(SG)],
                            [cacc[:, j, :] for j in range(2)])
                elif name == "sconv_split":
                    act.wait_ge(sconv_ready, l + 1)
                    nc.scalar.copy(sc_hi[:], gbT[:]).then_inc(mixh_ready, 1)
                elif name == "ssdT":
                    act.wait_ge(mixf_ready, 2 * l + 1)
                    nc.scalar.copy(h_hi[:, 4:8, :], ssd_mixf).then_inc(mixh_ready, 1)
                elif name == "soft":
                    n = P * (i % TT + 1)
                    act.wait_ge(sm_ready, NU * l + i + 1)
                    for m in range(2):
                        nc.scalar.activation(e_sb[:, i % 2, m, 0:n], s_sb[:, i % 2, m, 0:n], ACT.Exp,
                                             bias=nb[:, i % 2, m:m + 1], scale=HD ** -0.5,
                                             accum_out=es[:, i % 2, m:m + 1])
                    nc.scalar.drain().then_inc(e_ready, 1)
                elif name == "pt":
                    n = P * (i % TT + 1)
                    act.wait_ge(pt_done, NU * l + i + 1)
                    nc.scalar.copy(ptT[:, i % 2, 0:n], ps[:, 7, 0:n]).then_inc(pt_ready, 1)
                elif name == "pv":
                    h, t = i // TT, i % TT
                    r = rq(l, "attn")
                    act.wait_ge(pv_done, NU * l + i + 1)
                    o = ps[:, 7, 256:384]
                    nc.scalar.copy(o_tok[:, t, h * P:(h + 1) * P], o)
                    nc.scalar.activation(cacc[:, 1, 0:P], o, ACT.Square,
                                         accum_out=sumsq[:, r, t * HEADS + h:t * HEADS + h + 1])
                    nc.scalar.drain().then_inc(pv_out, 1)
                elif name == "attn":
                    nc.scalar.drain().then_inc(ss_ready, 1)
                    act.wait_ge(mixf_ready, 2 * l + 2)
                    nc.scalar.copy(h_hi[:, 0:4, :], att_mixf).then_inc(mixh_ready, 1)
                elif name == "grow":
                    act.wait_ge(grow_done, 2 * l + i + 1)
                    if i:
                        act.wait_ge(x_ready, 2 * l + 1)
                    elif l:
                        act.wait_ge(x_ready, 2 * l)
                    nc.scalar.copy(gate_row[:], pair(4 + 2 * i)).then_inc(grow_ready, 1)
                elif name == "post":
                    act.wait_ge(ysub_done, 2 * l + i + 1)
                    squares(l, ("post_mix", "post_ffn")[i], [pair(4 * i + 2 * t) for t in range(TT)], xn_scratch)
                elif name == "up":
                    act.wait_ge(f_up, i + 1)
                    if i:
                        act.wait_ge(f_ac, i)
                    nc.scalar.activation(f_silu[:], ps[:, 0, :].rearrange("p (j n) -> p j n", j=2),
                                         ACT.Silu).then_inc(f_sl, 1)
                elif name == "gate":
                    act.wait_ge(f_ac, i + 1)
                    nc.scalar.copy(f_hi[:, i % 2], f_act[:]).then_inc(f_h, 1)

            for g in range(4):
                act.wait_ge(htok_done, g + 1)
                nc.scalar.copy(ht_hi[:, g // 2, (g % 2) * 512:(g % 2 + 1) * 512], ps[:, 4 + g % 2, :]).then_inc(htok_h, 1)
            act.wait_ge(r_del, 1)
            nc.scalar.activation(led[:], ldel[:], ACT.Exp).then_inc(r_exp, 1)
            nc.scalar.mul(selgT[:], maskq[:, 0:1, :].to_broadcast([P, TT, P]), 0.0).then_inc(sgt_ready, 1)

            def gathered_hi(job):
                for g in range(2):
                    act.wait_ge(gat_done, job * 4 + (g + 1))
                    nc.scalar.copy(xe_hi[:, 4 * g:4 * g + 4, :],
                                   ps[:, FREE[g], :].rearrange("p (k n) -> p k n", k=4)).then_inc(xh_ready, 1)

            act.wait_ge(routed, 1)
            act.wait_ge(st_used, ND)
            n_jobs = act.value_load(njob[0:1, 0:1], min_val=NE, max_val=NJOB)
            gathered_hi(0)
            with act.Fori(0, n_jobs) as job:
                def split(i):
                    n = NS + i
                    act.wait_ge(landed[n % RING], job * (16 * JOB_SLOTS // RING) + 16 * (n // RING + 1))
                    act.wait_ge(st_used, job * JOB_SLOTS + (ND + i - JSTAGES + 1))
                    nc.scalar.copy(jst_hi[i % JSTAGES][:], ring[:, n % RING, :]).then_inc(hi_ready, 1)

                def silu(ch):
                    act.wait_ge(m_up, job * NCH + (ch + 1))
                    if ch:
                        act.wait_ge(m_ac, job * NCH + ch)
                    nc.scalar.activation(m_silu[:], ps[:, UPB, :], ACT.Silu).then_inc(m_sl, 1)

                def transposed(ch):
                    act.wait_ge(m_tp, job * NCH + (ch + 1))
                    nc.scalar.copy(a_hi[:], ps[:, TPB, :].rearrange("p (k n) -> p k n", k=4)).then_inc(m_th, 1)

                for i in range(3):
                    split(i)
                act.wait_ge(m_dn, job + 1)
                nc.scalar.copy(y_e[:], pair(YB)).then_inc(ye_out, 1)
                split(3)
                silu(0)
                for ch in range(1, NCH + 1):
                    o = 4 if ch == 1 else 6 * ch - 2
                    split(o)
                    split(o + 1)
                    if ch < NCH:
                        split(o + 2)
                        split(o + 3)
                        silu(ch)
                        transposed(ch - 1)
                        split(o + 4)
                        if ch == 1:
                            act.wait_ge(sgt_done, job + 1)
                            nc.scalar.copy(selgT[:], ps[:, 7, 0:TT * P].rearrange("p (t n) -> p t n", t=TT)).then_inc(sgt_ready, 1)
                        split(o + 5)
                    else:
                        transposed(ch - 1)
                        gathered_hi(job + 1)
            act.wait_ge(m_dn, n_jobs + 1)
            nc.scalar.copy(y_e[:], pair(YB)).then_inc(ye_out, 1)
            act.wait_ge(ysub_done, 2 * DEPTH)
            squares(DEPTH - 1, "post_ffn", [y_moe[:, t, :] for t in range(TT)], xn_scratch)

        @block.vector
        def _(dve):
            nc.vector.memset(praw[:], 0.0).then_inc(zeroed, 1)
            def per_head(a):
                return a.unsqueeze(2).to_broadcast([P, SH, SP_])

            def heads(a):
                return a.rearrange("p (h n) -> p h n", h=SH)

            def raw(a):
                return a.bitcast(F32)

            def norm(l, s):
                n = 2 * l + s
                for g in range(5):
                    if g < 4:
                        dve.wait_ge(xnT_ready, 4 * n + g + 1)
                        for j in range(2):
                            kt = 2 * g + j
                            nc.vector.tensor_scalar(hT[:, kt, :], ps[:, 4 + g % 2, j * SEQ:(j + 1) * SEQ],
                                                    acol[:, l, s, kt:kt + 1], modc[:, l, 3 * KT * s + kt:3 * KT * s + kt + 1],
                                                    ALU.mult, ALU.add)
                        nc.vector.drain().then_inc(hT_ready, 1)
                    if g:
                        k = slice(2 * g - 2, 2 * g)
                        dve.wait_ge(hh_ready, 4 * n + g)
                        nc.vector.tensor_tensor(h_lo[:, k, :], hT[:, k, :], raw(h_hi[:, k, :]), ALU.subtract).then_inc(hl_ready, 1)

            def normalised(l, s):
                r = rq(l, ("pre_mix", "pre_ffn")[s])
                dve.wait_ge(rstd_ready, r + 1)
                for t in range(TT):
                    nc.vector.tensor_scalar(xn[:, t, :], x_tok[:, t, :], rstd[:, r, t:t + 1], None, ALU.mult)
                nc.vector.drain().then_inc(xn_ready, 1)

            def post_norm(l, s, name, parts):
                r = rq(l, name)
                dve.wait_ge(rstd_ready, r + 1)
                dve.wait_ge(grow_ready, 2 * l + s + 1)
                for t in range(TT):
                    nc.vector.scalar_tensor_tensor(out=xn[:, t, :], in0=parts[t], scalar=rstd[:, r, t:t + 1],
                                                   in1=gate_row[:], op0=ALU.mult, op1=ALU.mult)
                nc.vector.drain()
                nc.vector.tensor_tensor(x_tok[:], x_tok[:], xn[:], ALU.add)
                nc.vector.drain().then_inc(x_ready, 1)

            n_split = n_macc = 0
            dve.wait_ge(c_ready, 1)
            for name, l, i in SCHED:
                if name == "split":
                    n, k = stream_of[n_split], n_split
                    dve.wait_ge(hi_ready, k + 1)
                    if k >= STAGES:
                        dve.wait_ge(st_used, k - STAGES + 1)
                    nc.vector.tensor_tensor(ring_lo[:, n % RING, :], ring[:, n % RING, :], raw(st_hi[k % STAGES][:]),
                                            ALU.subtract).then_inc(lo_ready, 1)
                    n_split += 1
                elif name == "mod":
                    n = stream_of_mod[n_macc]
                    dve.wait_ge(landed[n % RING], 16 * (n // RING + 1))
                    if n_macc >= 2:
                        dve.wait_ge(mcol_done, n_macc - 1)
                    w = ring[:, n % RING, :].rearrange("p (k n) -> p k n", k=KT)
                    acc = macc[:, n_macc % 2, :]
                    for k in range(KT):
                        if k:
                            nc.vector.drain()
                            nc.vector.scalar_tensor_tensor(out=acc, in0=w[:, k, :], scalar=c_act[:, k:k + 1], in1=acc,
                                                           op0=ALU.mult, op1=ALU.add)
                        else:
                            nc.vector.tensor_scalar(acc, w[:, k, :], c_act[:, k:k + 1], None, ALU.mult)
                    nc.vector.drain().then_inc(macc_ready, 1)
                    n_macc += 1
                elif name == "modfin":
                    a, b = (0, 2 * KT) if i == 0 else (2 * KT, NM)
                    by_dve, by_pools = mods_until(l, b // 2)
                    dve.wait_ge(mcol_done, by_dve)
                    if by_pools:
                        dve.wait_ge(pcol_done, by_pools)
                    nc.vector.tensor_tensor(modc[:, l, a:b], ps[:, mod_bank(l, a // 2), a:b],
                                            cols(0, ROW_BMOD + NM * l + a, b - a), ALU.add)
                    nc.vector.drain()
                    for s, (pre, post) in enumerate((("pre_mix", "post_mix"), ("pre_ffn", "post_ffn"))):
                        o = 3 * KT * s
                        if s == i:
                            nc.vector.scalar_tensor_tensor(out=acol[:, l, s], in0=modc[:, l, o + KT:o + 2 * KT], scalar=1.0,
                                                           in1=cols(1, GAIN[pre] + KT * l, KT), op0=ALU.add, op1=ALU.mult)
                        if i:
                            nc.vector.tensor_tensor(gcol[:, l, s], modc[:, l, o + 2 * KT:o + 3 * KT],
                                                    cols(1, GAIN[post] + KT * l, KT), ALU.mult)
                    nc.vector.drain().then_inc(mod_ready, 1)
                elif name == "xn":
                    normalised(l, i)
                elif name == "norm":
                    norm(l, i)
                elif name == "params":
                    dve.wait_ge(parT, 1)
                    nc.vector.tensor_copy(pcol[:], ps[:, 7, 0:3 * P])
                    nc.vector.drain().then_inc(pars, 1)
                    nc.vector.tensor_tensor(lamp[:], lamq[:, :, 0::2, :], lamq[:, :, 1::2, :], ALU.mult)
                    nc.vector.drain()
                    nc.vector.tensor_reduce(lams[:], lamp[:], AX.X, ALU.add).then_inc(lam_s, 1)
                    dve.wait_ge(lam_e, 1)
                    nc.vector.tensor_tensor(nlam[:], lame[:, :, 1], lame[:, :, 0], ALU.subtract)
                    nc.vector.drain()
                    for ll in range(DEPTH):
                        nc.vector.tensor_scalar(nlam[:, ll:ll + 1], nlam[:, ll:ll + 1], -lam_init(ll), None, ALU.add)
                        nc.vector.tensor_scalar(subc[:, ll:ll + 1], col(2, ROW_AS + ll), 1.0 - lam_init(ll), None, ALU.mult)
                    nc.vector.drain()
                elif name == "conv":
                    dve.wait_ge(proj_out, NOUT * l + i + 1)
                    if i == 0:
                        nc.vector.memset(xbcT[:, :, 0:PADX], 0.0)
                        nc.vector.drain()
                    if 4 * l + i > 0:
                        dve.wait_ge(conv_done, 4 * l + i)
                    for k in range(CCONV):
                        for j in range(2):
                            ct = 2 * i + j
                            w = col(1, ROW_CW + 8 * CCONV * l + 8 * k + ct)
                            if k == 0:
                                nc.vector.tensor_scalar(cacc[:, j, :], xbcT[:, ct, 0:SEQ], w,
                                                        col(2, ROW_CB + 8 * l + ct), ALU.mult, ALU.add)
                            else:
                                nc.vector.scalar_tensor_tensor(out=cacc[:, j, :], in0=xbcT[:, ct, k:k + SEQ], scalar=w,
                                                               in1=cacc[:, j, :], op0=ALU.mult, op1=ALU.add)
                        last = nc.vector.drain()
                    last.then_inc(conv_acc, 1)
                elif name == "dt":
                    dve.wait_ge(dt_mm, l + 1)
                    bias = small[:, DT_BIAS, SH * l:SH * (l + 1)].unsqueeze(1).to_broadcast([P, TT, SH])
                    nc.vector.tensor_tensor(dtr[:], ps[:, SSDB, DTC:DTC + TT * SH].rearrange("p (t h) -> p t h", t=TT),
                                            bias, ALU.add)
                    nc.vector.drain()
                    nc.vector.scalar_tensor_tensor(out=dta[:], in0=dtr[:], scalar=-1.0, in1=dtr[:], op0=ALU.mult, op1=ALU.min)
                    nc.vector.drain().then_inc(dt_a, 1)
                    nc.vector.tensor_scalar(dtr[:], dtr[:], 0.0, None, ALU.max)
                    dve.wait_ge(dt_e, 2 * l + 1)
                    nc.vector.tensor_scalar(dtu[:], dte_[:], 1.0, None, ALU.add)
                    nc.vector.drain().then_inc(dt_a, 1)
                    nc.vector.tensor_scalar(dtv[:], dtu[:], -1.0, None, ALU.add)
                    nc.vector.drain()
                    nc.vector.tensor_scalar(dtz[:], dtv[:], 0.0, None, ALU.is_equal)
                    nc.vector.drain()
                    nc.vector.tensor_tensor(dtv[:], dtv[:], dtz[:], ALU.add)
                    nc.vector.drain()
                    nc.vector.reciprocal(dtv[:], dtv[:])
                    nc.vector.tensor_tensor(dtz[:], dtz[:], dte_[:], ALU.mult)
                    nc.vector.drain()
                    nc.vector.tensor_tensor(dtv[:], dtv[:], dte_[:], ALU.mult)
                    nc.vector.tensor_tensor(dtr[:], dtr[:], dtz[:], ALU.add)
                    dve.wait_ge(dt_e, 2 * l + 2)
                    nc.vector.drain()
                    nc.vector.tensor_tensor(dtv[:], dtv[:], dtl[:], ALU.mult)
                    nc.vector.drain()
                    nc.vector.tensor_tensor(dtr[:], dtr[:], dtv[:], ALU.add)
                    nc.vector.drain()
                    an = aexp[:, SH * l:SH * (l + 1)].unsqueeze(1).to_broadcast([P, TT, SH])
                    nc.vector.scalar_tensor_tensor(out=dA[:], in0=dtr[:], scalar=-1.0, in1=an, op0=ALU.mult, op1=ALU.mult)
                    nc.vector.drain().then_inc(dt_ready, 1)
                elif name == "cum":
                    dve.wait_ge(cum_done, l + 1)
                    nc.vector.tensor_copy(acum[:], ps[:, SSDB, ACC:ACC + TT * SH].rearrange("p (t h) -> p t h", t=TT))
                    nc.vector.drain()
                    nc.vector.tensor_tensor(dsub[:], ps[:, SSDB, ALC:ALC + SH], acum[:, 0, :], ALU.subtract)
                    nc.vector.drain().then_inc(cum_sub, 1)
                elif name == "tok":
                    dve.wait_ge(tok_act, l + 1)
                    for t in range(TT):
                        nc.vector.tensor_tensor(heads(xdt[:, t, :]), heads(xs_tok[:, t, :]), per_head(dtr[:, t, :]), ALU.mult)
                    nc.vector.drain()
                    dve.wait_ge(cum_exp, l + 1)
                    nc.vector.tensor_tensor(heads(xdte[:]), heads(xdt[:, 0, :]), per_head(dend[:]), ALU.mult)
                    nc.vector.drain().then_inc(xdt_ready, 1)
                elif name == "decay":
                    dve.wait_ge(row_done, 2 * l + i + 1)
                    for h in range(SH):
                        nc.vector.scalar_tensor_tensor(out=decay[:, h, :], in0=pair(4)[:, h * P:(h + 1) * P],
                                                       scalar=acum[:, i, h:h + 1], in1=maskT[:],
                                                       op0=ALU.subtract, op1=ALU.add)
                    nc.vector.drain().then_inc(seg_ready, 1)
                    dve.wait_ge(dec_ready, 2 * l + i + 1)
                    for g in range(SG):
                        cb = ps[:, SSDB, CBC + g * P:CBC + (g + 1) * P].unsqueeze(1).to_broadcast([P, 4, P])
                        nc.vector.tensor_tensor(decay[:, 4 * g:4 * g + 4, :], decay[:, 4 * g:4 * g + 4, :], cb, ALU.mult)
                    nc.vector.drain().then_inc(mt_ready, 1)
                elif name == "ssd":
                    dskip = per_head(small[:, D_SKIP, SH * l:SH * (l + 1)])
                    nc.vector.tensor_tensor(heads(xs_tok[:, i, :]), heads(xs_tok[:, i, :]), dskip, ALU.mult)
                    dve.wait_ge(y_done, 2 * l + i + 1)
                    nc.vector.drain()
                    nc.vector.tensor_tensor(ytok[:, i, :], ps[:, 4, :], xs_tok[:, i, :], ALU.add)
                    if i == 1:
                        nc.vector.tensor_tensor(heads(xdt[:, 0, :]), heads(ps[:, 5, :]), per_head(eacum[:]), ALU.mult)
                        nc.vector.drain()
                        nc.vector.tensor_tensor(ytok[:, 1, :], ytok[:, 1, :], xdt[:, 0, :], ALU.add)
                    nc.vector.drain().then_inc(y_out, 1)
                elif name == "ssdnorm":
                    dve.wait_ge(proj_out, NOUT * l + NOUT_Z)
                    nc.vector.tensor_tensor(ytok, ytok, sz[:], ALU.mult)
                    nc.vector.drain().then_inc(v_ready, 1)
                    r = rq(l, "ssd")
                    dve.wait_ge(rstd_ready, r + 1)
                    for t in range(TT):
                        rs = rstd[:, r, t * SG:(t + 1) * SG].unsqueeze(2).to_broadcast([P, SG, 256])
                        yv = ytok[:, t, :].rearrange("p (g n) -> p g n", g=SG)
                        nc.vector.tensor_tensor(yv, yv, rs, ALU.mult)
                    nc.vector.drain().then_inc(vn_ready, 1)
                elif name == "sconv_split":
                    dve.wait_ge(mixh_ready, 3 * l + 1)
                    nc.vector.tensor_tensor(sc_lo[:], gbT[:], raw(sc_hi[:]), ALU.subtract).then_inc(mixl_ready, 1)
                elif name == "ssdT":
                    dve.wait_ge(ssdT, l + 1)
                    for j in range(4):
                        nc.vector.tensor_scalar(ssd_mixf[:, j, :], pair(4)[:, j * SEQ:(j + 1) * SEQ],
                                                col(2, ROW_SN + 4 * l + j), None, ALU.mult)
                    nc.vector.drain().then_inc(mixf_ready, 1)
                    dve.wait_ge(mixh_ready, 3 * l + 2)
                    nc.vector.tensor_tensor(h_lo[:, 4:8, :], ssd_mixf, raw(h_hi[:, 4:8, :]), ALU.subtract).then_inc(mixl_ready, 1)
                elif name == "soft":
                    t = i % TT
                    n = P * (t + 1)
                    b = i % 2
                    dve.wait_ge(sc_done, NU * l + i + 1)
                    if NU * l + i >= 2:
                        dve.wait_ge(e_ready, NU * l + i - 1)
                    sc = ps[:, 6, :].rearrange("p (m n) -> p m n", m=2)[:, :, 0:n]
                    mk = maskq[:].rearrange("p a n -> p (a n)")[:, SEQ - n:SEQ].unsqueeze(1).to_broadcast([P, 2, n])
                    nc.vector.tensor_tensor(s_sb[:, b, :, 0:n], sc, mk, ALU.add)
                    nc.vector.drain()
                    nc.vector.tensor_reduce(mx[:, b], s_sb[:, b, :, 0:n], AX.X, ALU.max)
                    nc.vector.drain()
                    nc.vector.tensor_scalar(nb[:, b], mx[:, b], -HD ** -0.5, None, ALU.mult)
                    nc.vector.drain().then_inc(sm_ready, 1)
                elif name == "pd":
                    n = P * (i % TT + 1)
                    b = i % 2
                    dve.wait_ge(e_ready, NU * l + i + 1)
                    nc.vector.reciprocal(er[:, b], es[:, b])
                    nc.vector.drain()
                    nc.vector.tensor_tensor(er[:, b, 1:2], er[:, b, 1:2], nlam[:, l:l + 1], ALU.mult)
                    nc.vector.tensor_scalar(e_sb[:, b, 0, 0:n], e_sb[:, b, 0, 0:n], er[:, b, 0:1], None, ALU.mult)
                    if NU * l + i >= 2:
                        dve.wait_ge(pt_done, NU * l + i - 1)
                    nc.vector.drain()
                    nc.vector.scalar_tensor_tensor(out=pd[:, b, 0:n], in0=e_sb[:, b, 1, 0:n], scalar=er[:, b, 1:2],
                                                   in1=e_sb[:, b, 0, 0:n], op0=ALU.mult, op1=ALU.add)
                    nc.vector.drain().then_inc(pd_ready, 1)
                elif name == "attn":
                    r = rq(l, "attn")
                    dve.wait_ge(rstd_ready, r + 1)
                    for t in range(TT):
                        rs = rstd[:, r, t * HEADS:(t + 1) * HEADS].unsqueeze(2).to_broadcast([P, HEADS, P])
                        ov = o_tok[:, t, :].rearrange("p (h n) -> p h n", h=HEADS)
                        nc.vector.tensor_tensor(ov, ov, rs, ALU.mult)
                    nc.vector.drain().then_inc(on_ready, 1)
                    dve.wait_ge(attT, l + 1)
                    for t in range(TT):
                        nc.vector.tensor_scalar(att_mixf[:, :, t * P:(t + 1) * P],
                                                ps[:, 6 + t, :].rearrange("p (h n) -> p h n", h=HEADS),
                                                subc[:, l:l + 1], None, ALU.mult)
                    nc.vector.drain().then_inc(mixf_ready, 1)
                    dve.wait_ge(mixh_ready, 3 * l + 3)
                    nc.vector.tensor_tensor(h_lo[:, 0:4, :], att_mixf, raw(h_hi[:, 0:4, :]), ALU.subtract).then_inc(mixl_ready, 1)
                elif name == "gate":
                    dve.wait_ge(f_sl, i + 1)
                    dve.wait_ge(f_gt, i + 1)
                    if i:
                        dve.wait_ge(f_h, i)
                        nc.vector.drain()
                    nc.vector.tensor_tensor(f_act[:], f_silu[:], ps[:, 1, :].rearrange("p (j n) -> p j n", j=2),
                                            ALU.mult).then_inc(f_ac, 1)
                    dve.wait_ge(f_h, i + 1)
                    nc.vector.tensor_tensor(f_lo[:, i % 2], f_act[:], raw(f_hi[:, i % 2]), ALU.subtract).then_inc(f_l, 1)
                elif name == "post":
                    post_norm(l, i, ("post_mix", "post_ffn")[i], [pair(4 * i + 2 * t) for t in range(TT)])

            nc.vector.memset(y_moe[:], 0.0)
            dve.wait_ge(lg_done, 1)
            nc.vector.tensor_copy(lg[:], ps[:, 6, 0:TT * NE].rearrange("p (t e) -> p t e", t=TT))
            nc.vector.drain()
            for t in range(TT):
                nc.vector.max(lmx[:, t, :], lg[:, t, :])
            nc.vector.drain()
            for t in range(TT):
                nc.vector.max_index(lix[:, t, :], lmx[:, t, :], lg[:, t, :])
            nc.vector.tensor_tensor(ldel[:], lmx[:, :, 1], lmx[:, :, 0], ALU.subtract)
            nc.vector.drain()
            nc.vector.tensor_copy(lixf[:], lix[:, :, 0:2])
            nc.vector.drain()
            for t in range(TT):
                nc.vector.tensor_scalar(oh1[:, t, :], iota[:, 0:NE], lixf[:, t, 0:1], None, ALU.is_equal)
                nc.vector.tensor_scalar(oh2[:, t, :], iota[:, 0:NE], lixf[:, t, 1:2], None, ALU.is_equal)
            nc.vector.drain()
            nc.vector.tensor_tensor(msk[:], oh1[:], oh2[:], ALU.add)
            nc.vector.drain().then_inc(r_del, 1)
            for g in range(4):
                s = slice((g % 2) * 512, (g % 2 + 1) * 512)
                dve.wait_ge(htok_h, g + 1)
                nc.vector.tensor_tensor(ht_lo[:, g // 2, s], ps[:, 4 + g % 2, :], raw(ht_hi[:, g // 2, s]),
                                        ALU.subtract).then_inc(htok_l, 1)
            dve.wait_ge(r_exp, 1)
            nc.vector.tensor_scalar(lden[:], led[:], 1.0, None, ALU.add)
            nc.vector.drain()
            nc.vector.reciprocal(lg1[:], lden[:])
            nc.vector.drain()
            nc.vector.tensor_tensor(lg2[:], lg1[:], led[:], ALU.mult)
            nc.vector.drain()
            for t in range(TT):
                nc.vector.tensor_scalar(oh2[:, t, :], oh2[:, t, :], lg2[:, t:t + 1], None, ALU.mult)
            nc.vector.drain()
            for t in range(TT):
                nc.vector.scalar_tensor_tensor(out=gts[:, t, :], in0=oh1[:, t, :], scalar=lg1[:, t:t + 1],
                                               in1=oh2[:, t, :], op0=ALU.mult, op1=ALU.add)
            dve.wait_ge(pos_done, 1)
            pos = ps[:, 6, 16:16 + TT * NE].rearrange("p (t e) -> p t e", t=TT)
            nc.vector.tensor_copy(posj[:, :, 0:NE], pos)
            nc.vector.tensor_copy(mskj[:, :, 0:NE], msk[:])
            nc.vector.tensor_copy(cnts[:], ps[:, 6, 32:32 + NE])
            nc.vector.tensor_copy(ejobf[:, 0:NE], iota[:, 0:NE])
            nc.vector.drain()
            nc.vector.tensor_copy(gtsj[:, :, 0:NE], gts[:])
            nc.vector.tensor_scalar(over[:], cnts[:], float(P), None, ALU.is_gt)
            nc.vector.drain()
            nc.vector.tensor_tensor_scan(ranki[:], ones[:, 0:NE], over[:], 0.0, ALU.mult, ALU.add)
            nc.vector.drain()
            nc.vector.tensor_tensor(rank[:], ranki[:], over[:], ALU.subtract)
            nc.vector.tensor_scalar(njf[:], ranki[:, NE - 1:NE], float(NE), None, ALU.add)
            nc.vector.drain()
            for k in range(EXTRA):
                nc.vector.scalar_tensor_tensor(out=ohk[:, k, :], in0=rank[:], scalar=float(k), in1=over[:],
                                               op0=ALU.is_equal, op1=ALU.mult)
            nc.vector.drain()
            nc.vector.tensor_tensor(epick[:], ohk[:], iota[:, 0:NE].unsqueeze(1).to_broadcast([P, EXTRA, NE]), ALU.mult)
            nc.vector.drain()
            nc.vector.tensor_reduce(ejobf[:, NE:NJOB], epick[:], AX.X, ALU.add)
            for table in (posj, mskj, gtsj):
                nc.vector.memset(table[:, :, NJOB:], 0.0)
                for t in range(TT):
                    nc.vector.tensor_tensor(pick[:, t], table[:, t, 0:NE].unsqueeze(1).to_broadcast([P, EXTRA, NE]),
                                            ohk[:], ALU.mult)
                nc.vector.drain()
                nc.vector.tensor_reduce(table[:, :, NE:NJOB], pick[:], AX.X, ALU.add)
                nc.vector.drain()
            nc.vector.tensor_scalar(posj[:, :, NE:NJOB], posj[:, :, NE:NJOB], -float(P), None, ALU.add)
            nc.vector.tensor_copy(ejob[:], ejobf[:])
            nc.vector.tensor_copy(njob[:], njf[:])
            nc.vector.drain().then_inc(routed, 1)

            dve.wait_ge(routed, 1)
            n_jobs = dve.value_load(njob[0:1, 0:1], min_val=NE, max_val=NJOB)

            def select(job, table_job):
                for t in range(TT):
                    one = lambda a: a[:, t, bass.ds(table_job, 1)]
                    nc.vector.tensor_scalar(sel[:, t, :], iota[:], one(posj), one(mskj), ALU.is_equal, ALU.mult)
                    nc.vector.tensor_scalar(selg[:, t, :], iota[:], one(posj), one(gtsj), ALU.is_equal, ALU.mult)
                nc.vector.drain().then_inc(sel_ready, 1)

            def gathered_lo(job):
                for g in range(2):
                    dve.wait_ge(gat_done, job * 4 + (g + 3))
                    nc.vector.tensor_copy(xe_lo[:, 4 * g:4 * g + 4, :],
                                          ps[:, FREE[2 + g], :].rearrange("p (k n) -> p k n", k=4)).then_inc(xl_ready, 1)

            def scattered(job):
                for g in range(4):
                    t, half = g // 2, g % 2
                    dve.wait_ge(sca_done, job * 4 + (g + 1))
                    y = y_moe[:, t, half * 512:(half + 1) * 512]
                    nc.vector.tensor_tensor(y, y, ps[:, FREE[g], :], ALU.add).then_inc(sca_out, 1)

            select(0, 0)
            gathered_lo(0)
            with dve.Fori(0, n_jobs) as job:
                def split(i):
                    n = NS + i
                    dve.wait_ge(hi_ready, job * JOB_SLOTS + (ND + i + 1))
                    nc.vector.tensor_tensor(ring_lo[:, n % RING, :], ring[:, n % RING, :], raw(jst_hi[i % JSTAGES][:]),
                                            ALU.subtract).then_inc(lo_ready, 1)

                def product(ch):
                    dve.wait_ge(m_sl, job * NCH + (ch + 1))
                    dve.wait_ge(m_gt, job * NCH + (ch + 1))
                    nc.vector.tensor_tensor(m_act[:, ch % 2, :], m_silu[:], ps[:, GATEB, :], ALU.mult).then_inc(m_ac, 1)

                def transposed(ch):
                    dve.wait_ge(m_th, job * NCH + (ch + 1))
                    nc.vector.tensor_tensor(a_lo[:], ps[:, TPB, :].rearrange("p (k n) -> p k n", k=4), raw(a_hi[:]),
                                            ALU.subtract).then_inc(m_tl, 1)

                for i in range(4):
                    split(i)
                for ch in range(1, NCH + 1):
                    o = 4 if ch == 1 else 6 * ch - 2
                    split(o)
                    product(ch - 1)
                    split(o + 1)
                    if ch == 1:
                        scattered(job)
                    if ch < NCH:
                        split(o + 2)
                        split(o + 3)
                        if ch == 4:
                            dve.wait_ge(sgt_done, job + 1)
                            select(job + 1, job + 1)
                        transposed(ch - 1)
                        split(o + 4)
                        split(o + 5)
                    else:
                        transposed(ch - 1)
                        gathered_lo(job + 1)
            scattered(n_jobs)
            nc.vector.drain().then_inc(ysub_done, 1)
            post_norm(DEPTH - 1, 1, "post_ffn", [y_moe[:, t, :] for t in range(TT)])

        @block.tensor
        def _(pe):
            used = [0]

            def weights(l, name, i):
                k = used[0]
                used[0] += 1
                pe.wait_ge(lo_ready, k + 1)
                a = staged_src[k].shape[1]
                return [s.rearrange("p (a b) -> p a b", a=a)
                        for s in (st_hi[k % STAGES][:], ring_lo[:, stream_of[k] % RING, :])]

            mm = nc.tensor.matmul

            def product(dst, left, right, start, stop):
                (lh, ll), (rh, rl) = left, right
                mm(dst, lh, rh, start=start, stop=False)
                mm(dst, lh, rl, start=False, stop=False)
                return mm(dst, ll, rh, start=False, stop=stop)

            pe.wait_ge(consts, 1)
            pe.wait_ge(zeroed, 1)

            def mix_parts(tile, t):
                s = slice(t * P, (t + 1) * P)
                if tile >= 8:
                    return sc_hi[:, tile - 8, s], sc_lo[:, tile - 8, s]
                return h_hi[:, tile, s], h_lo[:, tile, s]

            n_mcol = n_pcol = 0
            for name, l, i in SCHED:
                if name == "modcol":
                    b = mod_bank(l, i)
                    if i == 0 and l:
                        pe.wait_ge(x_ready, 2 * l - 1)
                    if i == FIRST_MOD and l == 0:
                        pe.wait_ge(mod_ready, 1)
                    if by_pool(l, i):
                        n_pcol += 1
                        pe.wait_ge(pacc_ready, n_pcol)
                        src, done = pacc, pcol_done
                    else:
                        n_mcol += 1
                        pe.wait_ge(macc_ready, n_mcol)
                        src, done = macc[:, (n_mcol - 1) % 2, :], mcol_done
                    for j in range(2):
                        last = mm(ps[:, b, 2 * i + j:2 * i + j + 1], src[:, j * P:(j + 1) * P], ones[:, 0:1],
                                  start=True, stop=True)
                    last.then_inc(done, 1)
                elif name == "params":
                    pe.wait_ge(par_landed, 17 * 16)
                    for j in range(3):
                        last = nc.tensor.transpose(ps[:, 7, j * P:(j + 1) * P], praw[:, j, :], ident[:])
                    last.then_inc(parT, 1)
                elif name == "norm":
                    n = 2 * l + i
                    pe.wait_ge(xn_ready, n + 1)
                    for g in range(4):
                        if g >= 2:
                            pe.wait_ge(hT_ready, 4 * n + g - 1)
                        for j in range(2):
                            for t in range(TT):
                                kt = 2 * g + j
                                last = nc.tensor.transpose(ps[:, 4 + g % 2, j * SEQ + t * P:j * SEQ + (t + 1) * P],
                                                           xn[:, t, kt * P:(kt + 1) * P], ident[:])
                        last.then_inc(xnT_ready, 1)
                    pe.wait_ge(hl_ready, 4 * n + 4)
                elif name == "out":
                    kind, half = OUTS[i]
                    n = NOUT * l + i
                    if kind in TOKEN_MAJOR:
                        if half == 0 and n:
                            pe.wait_ge(proj_out, n)
                        wh, wl = weights(l, name, i)
                        for t in range(TT):
                            for k in range(4):
                                kt = 4 * half + k
                                s = slice(t * P, (t + 1) * P)
                                last = product(ps[:, t, :], (h_hi[:, kt, s], h_lo[:, kt, s]), (wh[:, k, :], wl[:, k, :]),
                                               kt == 0, kt == KT - 1)
                        last.then_inc(st_used, 1)
                        if half:
                            nc.tensor.drain().then_inc(proj_done, 2)
                    else:
                        if n >= 2:
                            pe.wait_ge(proj_out, n - 1)
                        wh, wl = weights(l, name, i)
                        for j in range(2):
                            s = slice(j * P, (j + 1) * P)
                            for k in range(KT):
                                last = product(ps[:, i % 2, j * SEQ:(j + 1) * SEQ], (wh[:, k, s], wl[:, k, s]),
                                               (h_hi[:, k, :], h_lo[:, k, :]), k == 0, k == KT - 1)
                        last.then_inc(st_used, 1)
                        nc.tensor.drain().then_inc(proj_done, 1)
                elif name == "dt":
                    for t in range(TT):
                        for k in range(KT):
                            last = mm(ps[:, SSDB, DTC + SH * t:DTC + SH * (t + 1)], hT[:, k, t * P:(t + 1) * P], wdt[:, l, k, :],
                                      start=(k == 0), stop=(k == KT - 1))
                    last.then_inc(dt_mm, 1)
                elif name == "cum":
                    pe.wait_ge(dt_ready, l + 1)
                    for t in range(TT):
                        mm(ps[:, SSDB, ACC + SH * t:ACC + SH * (t + 1)], upper[:], dA[:, t, :], start=True, stop=True)
                    mm(ps[:, SSDB, ALC:ALC + SH], ones[:], dA[:, 0, :], start=True, stop=True).then_inc(cum_done, 1)
                elif name == "tok":
                    pe.wait_ge(conv_done, 4 * l + 4)
                    for t in range(TT):
                        for j in range(4):
                            nc.tensor.transpose(ps[:, 4 + t, j * P:(j + 1) * P], convT[:, j, t * P:(t + 1) * P], ident[:])
                    pe.wait_ge(cum_sub, l + 1)
                    for g in range(SG):
                        last = nc.tensor.transpose(ps[:, SSDB, CBC + g * P:CBC + (g + 1) * P], convT[:, 4 + g, 0:P], ident[:])
                    last.then_inc(tok_done, 1)
                elif name == "decay":
                    if i == 0:
                        pe.wait_ge(tok_act, l + 1)
                    else:
                        pe.wait_ge(y_out, 2 * l + 1)
                        pe.wait_ge(state_ready, l + 1)
                    for h in range(SH):
                        mm(pair(4)[:, h * P:(h + 1) * P], dA[:, i, h:h + 1].to_broadcast([P, P]), upper[:],
                           start=True, stop=True)
                    for g in range(SG):
                        last = mm(ps[:, SSDB, CBC + g * P:CBC + (g + 1) * P], convT[:, 4 + g, i * P:(i + 1) * P],
                                  convT[:, 6 + g, i * P:(i + 1) * P], start=True, stop=True)
                    last.then_inc(row_done, 1)
                elif name == "ssd":
                    pe.wait_ge(mt_ready, 2 * l + i + 1)
                    for h in range(SH):
                        mm(ps[:, 4, h * SP_:(h + 1) * SP_], decay[:, h, :], xdt[:, i, h * SP_:(h + 1) * SP_],
                           start=True, stop=True)
                    for g in range(SG):
                        w = slice(g * 256, (g + 1) * 256)
                        if i == 0:
                            last = mm(ps[:, 5, w], b_tok[:, g, :], xdte[:, w], start=True, stop=True)
                        else:
                            last = mm(ps[:, 5, w], convT[:, 6 + g, P:2 * P], prev[:, w], start=True, stop=True)
                    last.then_inc(y_done, 1)
                elif name == "ssdT":
                    pe.wait_ge(vn_ready, l + 1)
                    for j in range(4):
                        for t in range(TT):
                            last = nc.tensor.transpose(pair(4)[:, j * SEQ + t * P:j * SEQ + (t + 1) * P],
                                                       ytok[:, t, j * P:(j + 1) * P], ident[:])
                    last.then_inc(ssdT, 1)
                elif name == "soft":
                    h, t = i // TT, i % TT
                    n = P * (t + 1)
                    if i == 0:
                        pe.wait_ge(proj_out, NOUT * l + NOUT_V)
                    if NU * l + i >= 1:
                        pe.wait_ge(sm_ready, NU * l + i)
                    for m in range(2):
                        o = slice(m * HD, (m + 1) * HD)
                        if m:
                            nc.tensor.drain()
                        last = mm(ps[:, 6, m * SEQ:m * SEQ + n], qT[o, h, t * P:(t + 1) * P], kT[o, h, 0:n],
                                  start=True, stop=True)
                    last.then_inc(sc_done, 1)
                elif name == "pt":
                    pe.wait_ge(pd_ready, NU * l + i + 1)
                    if NU * l + i >= 1:
                        pe.wait_ge(pv_out, NU * l + i)
                    for k in range(i % TT + 1):
                        last = nc.tensor.transpose(ps[:, 7, k * P:(k + 1) * P], pd[:, i % 2, k * P:(k + 1) * P], ident[:])
                    last.then_inc(pt_done, 1)
                elif name == "pv":
                    h, t = i // TT, i % TT
                    pe.wait_ge(pt_ready, NU * l + i + 1)
                    for k in range(t + 1):
                        last = mm(ps[:, 7, 256:384], ptT[:, i % 2, k * P:(k + 1) * P], v_tok[:, k, h * P:(h + 1) * P],
                                  start=(k == 0), stop=(k == t))
                    last.then_inc(pv_done, 1)
                elif name == "attn":
                    pe.wait_ge(on_ready, l + 1)
                    for t in range(TT):
                        for h in range(HEADS):
                            last = nc.tensor.transpose(ps[:, 6 + t, h * P:(h + 1) * P], o_tok[:, t, h * P:(h + 1) * P], ident[:])
                    last.then_inc(attT, 1)
                elif name == "grow":
                    if i == 0:
                        pe.wait_ge(mod_ready, 2 * l + 2)
                        pe.wait_ge(mixf_ready, 2 * l + 1)
                    else:
                        pe.wait_ge(mixf_ready, 2 * l + 2)
                    for j in range(KT):
                        last = mm(pair(4 + 2 * i)[:, j * P:(j + 1) * P], gcol[:, l, i, j:j + 1].to_broadcast([P, P]),
                                  ident[:], start=True, stop=True)
                    last.then_inc(grow_done, 1)
                elif name == "wout":
                    r = WOUT_ORDER[i]
                    if i == 0:
                        pe.wait_ge(proj_out, NOUT * (l + 1))
                        pe.wait_ge(mod_ready, 2 * l + 2)
                        pe.wait_ge(mt_ready, 2 * l + 2)
                    if i % 2 == 0:
                        pe.wait_ge(mixl_ready, 3 * l + i // 2 + 1)
                    wh, wl = weights(l, name, i)
                    for k in range(2):
                        for t in range(TT):
                            for half in range(2):
                                s = slice(half * 512, (half + 1) * 512)
                                last = product(ps[:, 2 * t + half, :], mix_parts(2 * r + k, t), (wh[:, k, s], wl[:, k, s]),
                                               i == 0 and k == 0, i == 5 and k == 1)
                    last.then_inc(st_used, 1)
                    if i == 5:
                        nc.tensor.drain().then_inc(ysub_done, 1)
                elif name in ("up", "gate"):
                    b = 0 if name == "up" else 1
                    if i == 0 and b == 0:
                        pe.wait_ge(grow_ready, 2 * l + 2)
                    if i:
                        pe.wait_ge(f_ac if b else f_sl, i)
                    wh, wl = weights(l, name, i)
                    for j in range(2):
                        s = slice(j * P, (j + 1) * P)
                        for k in range(KT):
                            last = product(ps[:, b, j * SEQ:(j + 1) * SEQ], (wh[:, k, s], wl[:, k, s]),
                                           (h_hi[:, k, :], h_lo[:, k, :]), k == 0, k == KT - 1)
                    last.then_inc(st_used, 1)
                    nc.tensor.drain().then_inc(f_gt if b else f_up, 1)
                elif name == "down":
                    wh, wl = weights(l, name, i)
                    pe.wait_ge(f_l, i + 1)
                    for k in range(2):
                        for t in range(TT):
                            for half in range(2):
                                s, ts = slice(half * 512, (half + 1) * 512), slice(t * P, (t + 1) * P)
                                last = product(ps[:, 4 + 2 * t + half, :], (f_hi[:, i % 2, k, ts], f_lo[:, i % 2, k, ts]),
                                               (wh[:, k, s], wl[:, k, s]), i == 0 and k == 0, i == NQ - 1 and k == 1)
                    last.then_inc(st_used, 1)
                    if i == NQ - 1:
                        nc.tensor.drain().then_inc(ysub_done, 1)

            pe.wait_ge(grow_ready, 2 * DEPTH)
            for t in range(TT):
                for k in range(KT):
                    last = mm(ps[:, 6, t * NE:(t + 1) * NE], hT[:, k, t * P:(t + 1) * P], wrt[:, k, :],
                              start=(k == 0), stop=(k == KT - 1))
            last.then_inc(lg_done, 1)
            for g in range(4):
                if g >= 2:
                    pe.wait_ge(htok_l, g - 1)
                for k in range(4):
                    last = nc.tensor.transpose(ps[:, 4 + g % 2, k * P:(k + 1) * P],
                                               hT[:, (g % 2) * 4 + k, (g // 2) * P:(g // 2 + 1) * P], ident[:])
                last.then_inc(htok_done, 1)
                if g == 1:
                    pe.wait_ge(r_del, 1)
                    mm(ps[:, 6, 16:24], strict[:], msk[:, 0, :], start=True, stop=True)
                    mm(ps[:, 6, 24:32], ones[:], msk[:, 0, :], start=True, stop=False)
                    mm(ps[:, 6, 24:32], strict[:], msk[:, 1, :], start=False, stop=True)
                    mm(ps[:, 6, 32:40], ones[:], msk[:, 0, :], start=True, stop=False)
                    mm(ps[:, 6, 32:40], ones[:], msk[:, 1, :], start=False, stop=True).then_inc(pos_done, 1)
            pe.wait_ge(htok_l, 4)
            for half in range(2):
                last = mm(ps[:, YB + half, :], maskq[:, 0, :], y_moe[:, 0, 0:512], start=True, stop=True)
            last.then_inc(m_dn, 1)

            def gather(job):
                pe.wait_ge(sel_ready, job + 1)
                for g in range(4):
                    if g == 3:
                        pe.wait_ge(xh_ready, job * 2 + 1)
                    src = (ht_hi, ht_lo)[g // 2]
                    for k in range(4):
                        kt = 4 * (g % 2) + k
                        for t in range(TT):
                            last = mm(ps[:, FREE[g], k * P:(k + 1) * P], src[:, t, kt * P:(kt + 1) * P], sel[:, t, :],
                                      start=(t == 0), stop=(t == TT - 1))
                    last.then_inc(gat_done, 1)

            def scatter(job):
                pe.wait_ge(ye_out, job + 1)
                pe.wait_ge(sgt_ready, job + 1)
                for g in range(4):
                    t, half = g // 2, g % 2
                    if g == 3:
                        pe.wait_ge(sca_out, job * 4 + 1)
                    mm(ps[:, FREE[g], :], selgT[:, t, :], y_e[:, half * 512:(half + 1) * 512],
                       start=True, stop=True).then_inc(sca_done, 1)

            pe.wait_ge(routed, 1)
            n_jobs = pe.value_load(njob[0:1, 0:1], min_val=NE, max_val=NJOB)
            gather(0)
            with pe.Fori(0, n_jobs) as job:
                slot = [0]

                def job_weights(kind):
                    i = slot[0]
                    assert JOB[i][0] == kind
                    pe.wait_ge(lo_ready, job * JOB_SLOTS + (ND + i + 1))
                    slot[0] += 1
                    a = 2 if kind == "w2" else 4
                    return [s.rearrange("p (a b) -> p a b", a=a)
                            for s in (jst_hi[i % JSTAGES][:], ring_lo[:, (NS + i) % RING, :])]

                def transpose(ch):
                    pe.wait_ge(m_ac, job * NCH + (ch + 1))
                    for k in range(4):
                        last = nc.tensor.transpose(ps[:, TPB, k * P:(k + 1) * P], m_act[:, ch % 2, k * P:(k + 1) * P], ident[:])
                    last.then_inc(m_tp, 1)

                pe.wait_ge(xh_ready, job * 2 + 2)
                pe.wait_ge(xl_ready, job * 2 + 2)
                for ch in range(NCH + 1):
                    if ch < NCH:
                        for b, kind in ((UPB, "w1"), (GATEB, "w3")):
                            if ch:
                                pe.wait_ge(m_sl if b == UPB else m_ac, job * NCH + ch)
                            for kh in range(2):
                                wh, wl = job_weights(kind)
                                for k in range(4):
                                    kt = 4 * kh + k
                                    last = product(ps[:, b, :], (xe_hi[:, kt, :], xe_lo[:, kt, :]),
                                                   (wh[:, k, :], wl[:, k, :]), kt == 0, kt == KT - 1)
                                last.then_inc(st_used, 1)
                            nc.tensor.drain().then_inc(m_up if b == UPB else m_gt, 1)
                            if ch and b == UPB:
                                transpose(ch - 1)
                    if ch == 0:
                        scatter(job)
                    if ch == 1:
                        pe.wait_ge(sca_out, job * 4 + 3)
                        for t in range(TT):
                            last = nc.tensor.transpose(ps[:, 7, t * P:(t + 1) * P], selg[:, t, :], ident[:])
                        last.then_inc(sgt_done, 1)
                    if ch == NCH:
                        transpose(ch - 1)
                        pe.wait_ge(sca_out, job * 4 + 4)
                        pe.wait_ge(sgt_ready, job + 2)
                        gather(job + 1)
                    if ch:
                        pe.wait_ge(m_tl, job * NCH + ch)
                        for kh in range(2):
                            wh, wl = job_weights("w2")
                            for k in range(2):
                                for half in range(2):
                                    s = slice(half * 512, (half + 1) * 512)
                                    kk = 2 * kh + k
                                    last = product(ps[:, YB + half, :], (a_hi[:, kk, :], a_lo[:, kk, :]),
                                                   (wh[:, k, s], wl[:, k, s]), ch == 1 and kk == 0, ch == NCH and kk == 3)
                            last.then_inc(st_used, 1)
                nc.tensor.drain().then_inc(m_dn, 1)
            pe.wait_ge(xh_ready, n_jobs * 2 + 2)
            pe.wait_ge(xl_ready, n_jobs * 2 + 2)
            scatter(n_jobs)


_INS = ["x", "c", "w_mod", "b_mod", "norm_mix_pre", "norm_mix_post", "norm_ffn_pre", "norm_ffn_post",
        "w_in", "w_out", "lambda_qk", "attn_subln", "ssd_conv_w", "ssd_conv_b", "ssd_dt_bias",
        "ssd_a_log", "ssd_d", "ssd_norm", "sconv_w", "ffn_w1", "ffn_w3", "ffn_w2",
        "moe_router", "moe_w1", "moe_w3", "moe_w2"]
_OUTS = [((1, SEQ, D), "float32")]


def kernel(**inputs):
    import numpy as _np
    import concourse.bacc as _bacc
    from concourse import mybir as _mybir
    from concourse.bass_utils import run_bass_kernel_spmd as _run

    nc = _bacc.Bacc("TRN2", target_bir_lowering=False, num_devices=1)
    arrays, args = {}, []
    for name in _INS:
        a = _np.ascontiguousarray(inputs[name])
        arrays[f"in_{name}_dram"] = a
        args.append(nc.dram_tensor(f"in_{name}_dram", a.shape, _mybir.dt.from_np(a.dtype), kind="ExternalInput").ap())
    for i, (shape, dtype) in enumerate(_OUTS):
        dt = _mybir.dt.from_np(_np.dtype(dtype))
        args.append(nc.dram_tensor(f"out_{i}_dram", shape, dt, kind="ExternalOutput").ap())
    build(nc, *args)
    r = _run(nc, [arrays], core_ids=[0])
    return r.results[0]["out_0_dram"]
```
